# Optimizing a Trainium2 kernel written in Bass

```python
import jax, jax.numpy as jnp
from jax import lax
import numpy as np
import math

D_MODEL = 1024
BATCH = 1
SEQ = 256
DEPTH = 2

N_META = 16
GRID_W = 64
GLA_HEADS = 4
GLA_DK = 64
GLA_DV = 128
GLA_KEY = GLA_HEADS * GLA_DK
GLA_VAL = GLA_HEADS * GLA_DV
GLA_RANK = 16
GLA_TAU = 16.0
CHUNK = 64
ATT_HEADS = 8
ATT_KV_HEADS = 2
HEAD_DIM = 64
ATT_Q = ATT_HEADS * HEAD_DIM
ATT_KV = ATT_KV_HEADS * HEAD_DIM
Q_BLOCK = 128
ROPE_THETA = 10000.0
D_FF = 2816
EPS = 1e-6

IN_SIZES = (GLA_KEY, GLA_KEY, GLA_VAL, GLA_VAL, GLA_RANK, GLA_RANK,
            ATT_Q, ATT_KV, ATT_KV, D_MODEL, D_MODEL)
D_IN = sum(IN_SIZES)
SPLIT_POINTS = tuple(int(s) for s in np.cumsum(IN_SIZES)[:-1])


def rmsnorm(x, g):
    xf = x.astype(jnp.float32)
    y = xf * lax.rsqrt(jnp.mean(xf * xf, axis=-1, keepdims=True) + EPS)
    return (y * g.astype(jnp.float32)).astype(x.dtype)

def swiglu(x, w_gate, w_up, w_down):
    return (jax.nn.silu(x @ w_gate) * (x @ w_up)) @ w_down

def gla_causal_chunked(q, k, v, log_a):
    f32 = jnp.float32
    B, H, T, dk = q.shape
    dv = v.shape[-1]
    n = T // CHUNK
    qc = q.astype(f32).reshape(B, H, n, CHUNK, dk)
    kc = k.astype(f32).reshape(B, H, n, CHUNK, dk)
    vc = v.astype(f32).reshape(B, H, n, CHUNK, dv)
    bcum = jnp.cumsum(log_a.astype(f32).reshape(B, H, n, CHUNK, dk), axis=3)
    btot = bcum[:, :, :, -1:, :]
    q_dec = qc * jnp.exp(bcum)
    k_inv = kc * jnp.exp(-bcum)
    k_end = kc * jnp.exp(btot - bcum)
    mask = jnp.tril(jnp.ones((CHUNK, CHUNK), dtype=bool))
    att = jnp.where(mask, jnp.einsum('bhnid,bhnjd->bhnij', q_dec, k_inv), 0.0)
    o_intra = jnp.einsum('bhnij,bhnjv->bhniv', att, vc)
    kv_chunk = jnp.einsum('bhnjd,bhnjv->bhndv', k_end, vc)
    decay = jnp.exp(btot[:, :, :, 0, :])

    def step(S, inp):
        d, kv = inp
        return d[..., None] * S + kv, S

    S0 = jnp.zeros((B, H, dk, dv), f32)
    _, S_prev = lax.scan(step, S0, (jnp.moveaxis(decay, 2, 0), jnp.moveaxis(kv_chunk, 2, 0)))
    S_prev = jnp.moveaxis(S_prev, 0, 2)
    o_inter = jnp.einsum('bhnid,bhndv->bhniv', q_dec, S_prev)
    return (o_intra + o_inter).reshape(B, H, T, dv)

def gla_branch(q, k, v, r, lr_f, lr_b, w2, b2, gn_gain):
    B, L, _ = q.shape
    pad = CHUNK - N_META

    def heads(t, d):
        return t.reshape(B, L, GLA_HEADS, d).transpose(0, 2, 1, 3)

    def log_gate(lr, w, b):
        return jax.nn.log_sigmoid((lr @ w + b).astype(jnp.float32)) / GLA_TAU

    def padseq(t):
        return jnp.pad(t, ((0, 0), (0, 0), (pad, 0), (0, 0)))

    def flip(t):
        return jnp.flip(t, axis=2)

    qh = padseq(heads(q * GLA_DK ** -0.5, GLA_DK))
    kh = padseq(heads(k, GLA_DK))
    vh = padseq(heads(v, GLA_DV))
    gf = padseq(heads(log_gate(lr_f, w2[0], b2[0]), GLA_DK))
    gb = padseq(heads(log_gate(lr_b, w2[1], b2[1]), GLA_DK))
    o_f = gla_causal_chunked(qh, kh, vh, gf)
    o_b = flip(gla_causal_chunked(flip(qh), flip(kh), flip(vh), flip(gb)))
    o = (o_f + o_b)[:, :, pad:, :].transpose(0, 2, 1, 3)
    o = o * lax.rsqrt(jnp.mean(o * o, axis=-1, keepdims=True) + EPS)
    o = o.reshape(B, L, GLA_VAL) * gn_gain.astype(jnp.float32)
    return o.astype(r.dtype) * jax.nn.silu(r)

def axial_rope_tables(n_tok):
    f32 = jnp.float32
    rows = n_tok // GRID_W
    row = jnp.repeat(jnp.arange(rows), GRID_W).astype(f32)
    col = jnp.tile(jnp.arange(GRID_W), rows).astype(f32)
    axis_dim = HEAD_DIM // 2
    inv = ROPE_THETA ** (-jnp.arange(0, axis_dim, 2, dtype=f32) / axis_dim)
    ang = jnp.concatenate([row[:, None] * inv, col[:, None] * inv], axis=-1)
    ang = jnp.concatenate([jnp.zeros((N_META, axis_dim), f32), ang], axis=0)
    return jnp.cos(ang), jnp.sin(ang)

def apply_axial_rope(x, cos, sin):
    L = x.shape[-2]
    q4 = HEAD_DIM // 4
    xs = x.astype(jnp.float32).reshape(*x.shape[:-1], 2, 2, q4)
    x1, x2 = xs[..., 0, :], xs[..., 1, :]
    c = cos.reshape(L, 2, q4)
    s = sin.reshape(L, 2, q4)
    return jnp.stack([x1 * c - x2 * s, x2 * c + x1 * s], axis=-2).reshape(x.shape)

def attention_branch(q, k, v, gq, gk, cos, sin):
    B, L, _ = q.shape
    G = ATT_HEADS // ATT_KV_HEADS
    qh = q.reshape(B, L, ATT_KV_HEADS, G, HEAD_DIM).transpose(0, 2, 3, 1, 4)
    kh = k.reshape(B, L, ATT_KV_HEADS, HEAD_DIM).transpose(0, 2, 1, 3)
    vh = v.reshape(B, L, ATT_KV_HEADS, HEAD_DIM).transpose(0, 2, 1, 3)
    qh = apply_axial_rope(rmsnorm(qh, gq), cos, sin) * HEAD_DIM ** -0.5
    kh = apply_axial_rope(rmsnorm(kh, gk), cos, sin)
    pad = Q_BLOCK - N_META
    qp = jnp.pad(qh, ((0, 0), (0, 0), (0, 0), (pad, 0), (0, 0)))
    nblk = qp.shape[3] // Q_BLOCK
    qb = jnp.moveaxis(qp.reshape(B, ATT_KV_HEADS, G, nblk, Q_BLOCK, HEAD_DIM), 3, 0)

    def block(qblk):
        s = jnp.einsum('bkgqd,bksd->bkgqs', qblk, kh)
        p = jax.nn.softmax(s, axis=-1)
        return jnp.einsum('bkgqs,bksd->bkgqd', p.astype(vh.dtype), vh)

    o = lax.map(block, qb)
    o = jnp.moveaxis(o, 0, 3).reshape(B, ATT_KV_HEADS, G, nblk * Q_BLOCK, HEAD_DIM)[:, :, :, pad:]
    return o.transpose(0, 3, 1, 2, 4).reshape(B, L, ATT_Q).astype(q.dtype)

def mixer(z, w_in, gla_w2, gla_b2, gla_gn, q_norm, k_norm, w_pa, w_pb, b_merge, w_out, cos, sin):
    h = z @ w_in
    (q_a, k_a, v_a, r_a, lr_f, lr_b, q_b, k_b, v_b, g_a, g_b) = jnp.split(h, SPLIT_POINTS, axis=-1)
    a = gla_branch(q_a, k_a, v_a, r_a, lr_f, lr_b, gla_w2, gla_b2, gla_gn)
    b = attention_branch(q_b, k_b, v_b, q_norm, k_norm, cos, sin)
    y = (jax.nn.sigmoid(g_a + b_merge[0]) * (a @ w_pa)
         + jax.nn.sigmoid(g_b + b_merge[1]) * (b @ w_pb))
    return y @ w_out

def first_inputs(seed: int = 0) -> dict:
    key = jax.random.key(seed)
    ks = jax.random.split(key, 18)

    def nrm(k, shape, scale):
        return jax.random.normal(k, shape, jnp.float32) * scale

    return {
        "x": nrm(ks[0], (BATCH, SEQ, D_MODEL), 1.0),
        "meta_tokens": nrm(ks[1], (N_META, D_MODEL), 1.0),
        "norm_gains": 1.0 + nrm(ks[2], (DEPTH, 3, D_MODEL), 0.02),
        "ffn_w_gate": nrm(ks[3], (DEPTH, 2, D_MODEL, D_FF), D_MODEL ** -0.5),
        "ffn_w_up": nrm(ks[4], (DEPTH, 2, D_MODEL, D_FF), D_MODEL ** -0.5),
        "ffn_w_down": nrm(ks[5], (DEPTH, 2, D_FF, D_MODEL), D_FF ** -0.5),
        "w_in": nrm(ks[6], (DEPTH, D_MODEL, D_IN), D_MODEL ** -0.5),
        "gla_w2": nrm(ks[7], (DEPTH, 2, GLA_RANK, GLA_KEY), GLA_RANK ** -0.5),
        "gla_b2": nrm(ks[8], (DEPTH, 2, GLA_KEY), 0.1),
        "gla_gn": 1.0 + nrm(ks[9], (DEPTH, GLA_VAL), 0.02),
        "q_norm": 1.0 + nrm(ks[10], (DEPTH, HEAD_DIM), 0.02),
        "k_norm": 1.0 + nrm(ks[11], (DEPTH, HEAD_DIM), 0.02),
        "w_pa": nrm(ks[12], (DEPTH, GLA_VAL, D_MODEL), GLA_VAL ** -0.5),
        "w_pb": nrm(ks[13], (DEPTH, ATT_Q, D_MODEL), ATT_Q ** -0.5),
        "b_merge": nrm(ks[14], (DEPTH, 2, D_MODEL), 0.02),
        "w_out": nrm(ks[15], (DEPTH, D_MODEL, D_MODEL), D_MODEL ** -0.5),
        "final_norm": 1.0 + nrm(ks[16], (D_MODEL,), 0.02),
    }

def first_block(x, meta_tokens, norm_gains, ffn_w_gate, ffn_w_up, ffn_w_down, w_in, gla_w2, gla_b2,
              gla_gn, q_norm, k_norm, w_pa, w_pb, b_merge, w_out, final_norm):
    B, N, D = x.shape
    meta = jnp.broadcast_to(meta_tokens[None].astype(x.dtype), (B, N_META, D))
    h = jnp.concatenate([meta, x], axis=1)
    cos, sin = axial_rope_tables(N)
    for l in range(DEPTH):
        h = h + 0.5 * swiglu(rmsnorm(h, norm_gains[l, 0]),
                             ffn_w_gate[l, 0], ffn_w_up[l, 0], ffn_w_down[l, 0])
        h = h + mixer(rmsnorm(h, norm_gains[l, 1]), w_in[l], gla_w2[l], gla_b2[l], gla_gn[l],
                      q_norm[l], k_norm[l], w_pa[l], w_pb[l], b_merge[l], w_out[l], cos, sin)
        h = h + 0.5 * swiglu(rmsnorm(h, norm_gains[l, 2]),
                             ffn_w_gate[l, 1], ffn_w_up[l, 1], ffn_w_down[l, 1])
    return rmsnorm(h, final_norm)[:, N_META:]


N_MIXERS = 2
N_CONV_LAYERS = (DEPTH + N_MIXERS - 1) // N_MIXERS
N_ATTN_LAYERS = DEPTH // N_MIXERS
CONV_WIDTH = 3
N_HEADS = 16
KV_LATENT = 128
N_IDX_HEADS = 8
IDX_DIM = 64
TOPK_MAX = 256
ATTN_IN_WIDTH = N_HEADS * KV_LATENT + KV_LATENT + N_IDX_HEADS * IDX_DIM + IDX_DIM + N_IDX_HEADS
N_BUCKETS = 32
MAX_DISTANCE = 128
N_GROUPS = 8
EXPERTS_PER_GROUP = 8
N_EXPERTS = N_GROUPS * EXPERTS_PER_GROUP
TOPK_IN_GROUP = 2
D_EXPERT = 256
MOE_BLOCK = 128
LN_EPS = 1e-5
RMS_EPS = 1e-6
DEEPNORM_ALPHA = (2.0 * DEPTH) ** 0.25
DEEPNORM_BETA = (8.0 * DEPTH) ** -0.25


def layer_norm(x, g, b):
    xf = x.astype(jnp.float32)
    mu = jnp.mean(xf, axis=-1, keepdims=True)
    var = jnp.mean(jnp.square(xf - mu), axis=-1, keepdims=True)
    y = (xf - mu) * lax.rsqrt(var + LN_EPS) * g.astype(jnp.float32) + b.astype(jnp.float32)
    return y.astype(x.dtype)

def rms_norm(x, g):
    xf = x.astype(jnp.float32)
    y = xf * lax.rsqrt(jnp.mean(jnp.square(xf), axis=-1, keepdims=True) + RMS_EPS) * g.astype(jnp.float32)
    return y.astype(x.dtype)

def t5_bucket(dist):
    max_exact = N_BUCKETS // 2
    d_f = jnp.maximum(dist, 1).astype(jnp.float32)
    large = max_exact + (jnp.log(d_f / max_exact) / math.log(MAX_DISTANCE / max_exact)
                         * (N_BUCKETS - max_exact)).astype(jnp.int32)
    large = jnp.minimum(large, N_BUCKETS - 1)
    return jnp.where(dist < max_exact, dist, large)

def short_conv_mixer(x, w_in, conv_k, w_out):
    S = x.shape[1]
    b_gate, c_gate, h = jnp.split(x @ w_in, 3, axis=-1)
    u = c_gate * h
    up = jnp.pad(u, ((0, 0), (CONV_WIDTH - 1, 0), (0, 0)))
    conv = up[:, 0:S] * conv_k[0]
    for j in range(1, CONV_WIDTH):
        conv = conv + up[:, j:j + S] * conv_k[j]
    return (b_gate * conv) @ w_out

def dsa_mixer(x, w_in, kv_norm_g, kidx_ln_g, kidx_ln_b, w_out, rel_bias):
    Bsz, S, _ = x.shape
    topk = min(TOPK_MAX, S // 4)
    hq = N_HEADS * KV_LATENT
    cuts = [hq, hq + KV_LATENT, hq + KV_LATENT + N_IDX_HEADS * IDX_DIM,
            hq + KV_LATENT + N_IDX_HEADS * IDX_DIM + IDX_DIM]
    q, c_kv, q_idx, k_idx, w_idx = jnp.split(x @ w_in, cuts, axis=-1)
    q = q.reshape(Bsz, S, N_HEADS, KV_LATENT)
    c_kv = rms_norm(c_kv, kv_norm_g)
    q_idx = q_idx.reshape(Bsz, S, N_IDX_HEADS, IDX_DIM)
    k_idx = layer_norm(k_idx, kidx_ln_g, kidx_ln_b)
    w_idx = w_idx * (N_IDX_HEADS ** -0.5)
    nb = S // Q_BLOCK
    key_pos = jnp.arange(S)

    def to_blocks(a):
        return jnp.moveaxis(a.reshape(Bsz, nb, Q_BLOCK, *a.shape[2:]), 1, 0)

    def block_fn(args):
        qb, qib, wb, blk = args
        t = blk * Q_BLOCK + jnp.arange(Q_BLOCK)
        s_idx = jnp.einsum('bthd,bsd->bths', qib, k_idx,
                           preferred_element_type=jnp.float32) * (IDX_DIM ** -0.5)
        score = jnp.einsum('bths,bth->bts', jax.nn.relu(s_idx), wb.astype(jnp.float32))
        causal = key_pos[None, :] <= t[:, None]
        score = jnp.where(causal[None], score, -jnp.inf)
        _, sel = lax.top_k(score, topk)
        valid = sel <= t[None, :, None]
        kv_sel = jax.vmap(lambda c, i: c[i])(c_kv, sel)
        logits = jnp.einsum('bthc,btjc->bthj', qb, kv_sel,
                            preferred_element_type=jnp.float32) * (KV_LATENT ** -0.5)
        bucket = t5_bucket(jnp.maximum(t[None, :, None] - sel, 0))
        bias = jnp.moveaxis(rel_bias[bucket], -1, 2)
        logits = logits + bias.astype(jnp.float32)
        logits = jnp.where(valid[:, :, None, :], logits, -jnp.inf)
        p = jax.nn.softmax(logits, axis=-1).astype(x.dtype)
        o = jnp.einsum('bthj,btjc->bthc', p, kv_sel)
        return o.reshape(Bsz, Q_BLOCK, hq)

    o = lax.map(block_fn, (to_blocks(q), to_blocks(q_idx), to_blocks(w_idx), jnp.arange(nb)))
    o = jnp.moveaxis(o, 0, 1).reshape(Bsz, S, hq)
    return o @ w_out

def hier_moe(x, wg, bg, we, be, w1, w3, w2):
    Bsz, S, D = x.shape
    xt = x.reshape(-1, D)
    T = xt.shape[0]
    g_logits = (xt @ wg + bg).astype(jnp.float32)
    g_prob = jax.nn.softmax(g_logits, axis=-1)
    g_top = jnp.argmax(g_logits, axis=-1)
    g_gate = jnp.take_along_axis(g_prob, g_top[:, None], axis=-1)
    e_logits = (xt @ we + be).astype(jnp.float32).reshape(T, N_GROUPS, EXPERTS_PER_GROUP)
    e_logits = jnp.take_along_axis(e_logits, g_top[:, None, None], axis=1)[:, 0]
    e_val, e_loc = lax.top_k(e_logits, TOPK_IN_GROUP)
    gate = jax.nn.softmax(e_val, axis=-1) * g_gate
    e_id = g_top[:, None] * EXPERTS_PER_GROUP + e_loc
    N = T * TOPK_IN_GROUP
    flat_e = e_id.reshape(-1).astype(jnp.int32)
    flat_tok = jnp.repeat(jnp.arange(T, dtype=jnp.int32), TOPK_IN_GROUP)
    flat_w = gate.reshape(-1)
    order = jnp.argsort(flat_e)
    e_s, tok_s, w_s = flat_e[order], flat_tok[order], flat_w[order]
    counts = jax.ops.segment_sum(jnp.ones_like(flat_e), flat_e, num_segments=N_EXPERTS)
    padded = (counts + MOE_BLOCK - 1) // MOE_BLOCK * MOE_BLOCK
    start = jnp.cumsum(counts) - counts
    pend = jnp.cumsum(padded)
    pstart = pend - padded
    dest = pstart[e_s] + jnp.arange(N, dtype=jnp.int32) - start[e_s]
    R = (-(-N // MOE_BLOCK) + N_EXPERTS) * MOE_BLOCK
    row_tok = jnp.zeros((R,), jnp.int32).at[dest].set(tok_s)
    row_w = jnp.zeros((R,), jnp.float32).at[dest].set(w_s)
    nblk = R // MOE_BLOCK
    blk_e = jnp.minimum(jnp.searchsorted(pend, jnp.arange(nblk, dtype=jnp.int32) * MOE_BLOCK,
                                         side='right'), N_EXPERTS - 1)
    xs = xt[row_tok].reshape(nblk, MOE_BLOCK, D)

    def expert_block(args):
        xb, e = args
        h = jax.nn.silu(xb @ w1[e]) * (xb @ w3[e])
        return h @ w2[e]

    ys = lax.map(expert_block, (xs, blk_e)).reshape(R, D)
    out = jnp.zeros_like(xt).at[row_tok].add(ys * row_w[:, None].astype(ys.dtype))
    return out.reshape(Bsz, S, D)

def second_inputs(seed: int = 0) -> dict:
    key = jax.random.key(seed)
    ks = jax.random.split(key, 24)
    D = D_MODEL
    f32 = jnp.float32

    def nrm(k, shape, scale):
        return jax.random.normal(k, shape, f32) * scale

    return {
        "x": nrm(ks[0], (BATCH, SEQ, D), 1.0),
        "conv_w_in": nrm(ks[1], (N_CONV_LAYERS, D, 3 * D), D ** -0.5),
        "conv_k": nrm(ks[2], (N_CONV_LAYERS, CONV_WIDTH, D), CONV_WIDTH ** -0.5),
        "conv_w_out": nrm(ks[3], (N_CONV_LAYERS, D, D), DEEPNORM_BETA * D ** -0.5),
        "attn_w_in": nrm(ks[4], (N_ATTN_LAYERS, D, ATTN_IN_WIDTH), D ** -0.5),
        "kv_norm_g": 1.0 + nrm(ks[5], (N_ATTN_LAYERS, KV_LATENT), 0.02),
        "kidx_ln_g": 1.0 + nrm(ks[6], (N_ATTN_LAYERS, IDX_DIM), 0.02),
        "kidx_ln_b": nrm(ks[7], (N_ATTN_LAYERS, IDX_DIM), 0.02),
        "attn_w_out": nrm(ks[8], (N_ATTN_LAYERS, N_HEADS * KV_LATENT, D),
                          DEEPNORM_BETA * (N_HEADS * KV_LATENT) ** -0.5),
        "rel_bias": nrm(ks[9], (N_BUCKETS, N_HEADS), 0.5),
        "router_wg": nrm(ks[10], (DEPTH, D, N_GROUPS), D ** -0.5),
        "router_bg": nrm(ks[11], (DEPTH, N_GROUPS), 0.01),
        "router_we": nrm(ks[12], (DEPTH, D, N_EXPERTS), D ** -0.5),
        "router_be": nrm(ks[13], (DEPTH, N_EXPERTS), 0.01),
        "exp_w1": nrm(ks[14], (DEPTH, N_EXPERTS, D, D_EXPERT), D ** -0.5),
        "exp_w3": nrm(ks[15], (DEPTH, N_EXPERTS, D, D_EXPERT), D ** -0.5),
        "exp_w2": nrm(ks[16], (DEPTH, N_EXPERTS, D_EXPERT, D), DEEPNORM_BETA * D_EXPERT ** -0.5),
        "ln1_g": 1.0 + nrm(ks[17], (DEPTH, D), 0.02),
        "ln1_b": nrm(ks[18], (DEPTH, D), 0.02),
        "ln2_g": 1.0 + nrm(ks[19], (DEPTH, D), 0.02),
        "ln2_b": nrm(ks[20], (DEPTH, D), 0.02),
    }

def second_block(x, conv_w_in, conv_k, conv_w_out, attn_w_in, kv_norm_g, kidx_ln_g, kidx_ln_b,
              attn_w_out, rel_bias, router_wg, router_bg, router_we, router_be,
              exp_w1, exp_w3, exp_w2, ln1_g, ln1_b, ln2_g, ln2_b):
    for i in range(DEPTH):
        j = i // N_MIXERS
        if i % N_MIXERS == 0:
            m = short_conv_mixer(x, conv_w_in[j], conv_k[j], conv_w_out[j])
        else:
            m = dsa_mixer(x, attn_w_in[j], kv_norm_g[j], kidx_ln_g[j], kidx_ln_b[j],
                          attn_w_out[j], rel_bias)
        x = layer_norm(DEEPNORM_ALPHA * x + m, ln1_g[i], ln1_b[i])
        f = hier_moe(x, router_wg[i], router_bg[i], router_we[i], router_be[i],
                     exp_w1[i], exp_w3[i], exp_w2[i])
        x = layer_norm(DEEPNORM_ALPHA * x + f, ln2_g[i], ln2_b[i])
    return x


def setup_inputs(seed=0):
    out = dict(first_inputs(seed))
    for name, value in second_inputs(seed + 1).items():
        if name != "x":
            out[name + "_2"] = value
    return out


def reference(
    x, meta_tokens, norm_gains, ffn_w_gate, ffn_w_up, ffn_w_down, w_in, gla_w2, gla_b2, gla_gn,
    q_norm, k_norm, w_pa, w_pb, b_merge, w_out, final_norm, conv_w_in_2, conv_k_2, conv_w_out_2,
    attn_w_in_2, kv_norm_g_2, kidx_ln_g_2, kidx_ln_b_2, attn_w_out_2, rel_bias_2, router_wg_2,
    router_bg_2, router_we_2, router_be_2, exp_w1_2, exp_w3_2, exp_w2_2, ln1_g_2, ln1_b_2,
    ln2_g_2, ln2_b_2,
):
    x = first_block(
        x, meta_tokens, norm_gains, ffn_w_gate, ffn_w_up, ffn_w_down, w_in, gla_w2, gla_b2,
        gla_gn, q_norm, k_norm, w_pa, w_pb, b_merge, w_out, final_norm,
    )
    return second_block(
        x, conv_w_in_2, conv_k_2, conv_w_out_2, attn_w_in_2, kv_norm_g_2, kidx_ln_g_2,
        kidx_ln_b_2, attn_w_out_2, rel_bias_2, router_wg_2, router_bg_2, router_we_2,
        router_be_2, exp_w1_2, exp_w3_2, exp_w2_2, ln1_g_2, ln1_b_2, ln2_g_2, ln2_b_2,
    )


_drawn_inputs = setup_inputs


def setup_inputs(seed=0):
    import zlib

    import numpy as np

    out = dict(_drawn_inputs(seed))
    spreads = {}
    factors = {'gla_gn': 3.408,
     'q_norm': 8.0,
     'k_norm': 8.0,
     'b_merge': 7.234,
     'kv_norm_g_2': 8.0,
     'kidx_ln_g_2': 6.977,
     'kidx_ln_b_2': 8.0,
     'router_bg_2': 8.0,
     'router_be_2': 8.0}
    for name, (base, spread) in spreads.items():
        noise = np.random.default_rng([zlib.crc32(name.encode()), seed]).standard_normal(out[name].shape)
        drawn = base * np.exp(spread * noise) if base else spread * noise
        out[name] = __import__('jax').numpy.asarray(drawn.astype(out[name].dtype))
    for name, factor in factors.items():
        out[name] = (out[name] * factor).astype(out[name].dtype)
    return out
```

```python
from contextlib import ExitStack

import numpy as np

import concourse.bass as bass
from concourse import mybir

ALU = mybir.AluOpType
ACT = mybir.ActivationFunctionType
AX = mybir.AxisListType
F32 = mybir.dt.float32
I32 = mybir.dt.int32

P = 128
D = 1024
KD = D // P
SEQ, META = 256, 16
T = SEQ + META
TILES = [(0, 128), (128, 128), (256, 16)]
FF = 2816
NF = FF // P
EPS_RMS, EPS_LN = 1e-6, 1e-5
C_QA, C_KA, C_VA, C_RA, C_LF, C_LB, C_QB, C_KB, C_VB, C_GA, C_GB = (
    0, 256, 512, 1024, 1536, 1552, 1568, 2080, 2208, 2336, 3360)
C_Q2, C_CKV, C_QI, C_KI, C_WI, C_END2 = 0, 2048, 2176, 2688, 2752, 2760
NH2 = 16
TOPK = 64
ALPHA = 4.0 ** 0.25
BIG = 1.0e30
LOWEST = -3.0e38
NE = 64
SLOTS = 32
MORE = 16
NBLK = NE + MORE
GROUP = 4
NG0, NG = NE // GROUP, NBLK // GROUP
RING = 4
SLOT = 4096


class Layout:

    def __init__(self):
        self.at, self.n = {}, 0

    def add(self, name, n):
        self.at[name] = (self.n, n)
        self.n += n

    def __call__(self, buf, name, rows=P):
        a, n = self.at[name]
        return buf[0:rows, a:a + n]


def const_layout():
    c = Layout()
    for name, n in (("ident", 128), ("ones", 128), ("mean_d", 128), ("mean128", 128), ("mean64", 128),
                    ("swap", 128), ("before", 128), ("sum4", 32), ("low", 64), ("high", 64),
                    ("cos", T), ("sin", T), ("cosq", T), ("sinq", T), ("restart", T),
                    ("causal", 512), ("future", 512), ("onehot", 384), ("rev8", 8), ("steps8", 8), ("iota", 128),
                    ("row32", 1), ("eps_rms", 1), ("eps_ln", 1), ("one", 64), ("blocks", MORE), ("first", NE), ("late", NE), ("groups", 4)):
        c.add(name, n)
    return c


def small_layout():
    s = Layout()
    for name, n in (("gains", 48), ("final", 8), ("gla_b", 8), ("gla_gn", 8), ("qn", 2), ("kn", 2),
                    ("bmerge", 32), ("convk", 24), ("kvg", 1), ("kig", 1), ("kib", 1), ("rb", 144),
                    ("ln1g", 16), ("ln1b", 16), ("ln2g", 16), ("ln2b", 16), ("rel", NH2), ("gla_w", 512)):
        s.add(name, n)
    return s


def constants():
    c = const_layout()
    out = np.zeros((P, c.n), np.float32)

    def put(name, v):
        a, n = c.at[name]
        v = np.asarray(v, np.float32)
        out[:v.shape[0], a:a + n] = v

    p = np.arange(P)
    put("ident", np.eye(P))
    put("ones", np.ones((P, P)))
    put("mean_d", np.full((P, P), 1.0 / D))
    put("mean128", np.full((P, P), 1.0 / 128))
    put("mean64", (p[:, None] // 64 == p[None] // 64) / 64.0)
    sw = np.zeros((P, P))
    for m in range(P):
        if m % 32 < 16:
            sw[m + 16, m] = -1.0
        else:
            sw[m - 16, m] = 1.0
    put("swap", sw)
    put("before", p[:, None] < p[None])
    put("sum4", (p[:, None] % 32) == np.arange(32)[None])
    put("low", (p[:, None] % 64) <= np.arange(64)[None])
    put("high", (p[:, None] % 64) >= np.arange(64)[None])
    inv = np.float32(10000.0) ** (-np.arange(0, 32, 2, dtype=np.float32) / np.float32(32))
    tok = np.arange(SEQ)
    ang = np.zeros((P, T), np.float32)
    for m in range(P):
        pos = tok // 64 if (m % 64) < 32 else tok % 64
        ang[m, :SEQ] = pos.astype(np.float32) * inv[m % 16]
    put("cos", np.cos(ang))
    put("sin", np.sin(ang))
    put("cosq", np.cos(ang) * np.float32(0.125))
    put("sinq", np.sin(ang) * np.float32(0.125))
    rs = np.ones((P, T))
    rs[:, [0, 64, 128, 192, 256]] = 0
    put("restart", rs)
    t = np.concatenate([p, p + 128]).reshape(2, P).T
    s = np.arange(SEQ)
    causal = (s[None, None] <= t[:, :, None]).astype(np.float32)
    put("causal", causal.reshape(P, 512))
    put("future", ((1 - causal) * np.float32(-BIG)).reshape(P, 512))
    dist = np.maximum(255 - np.arange(384), 0)
    f = np.maximum(dist, 1).astype(np.float32)
    large = 16 + (np.log(f / np.float32(16)) / np.float32(np.log(8.0)) * np.float32(16)).astype(np.int32)
    bucket = np.where(dist < 16, dist, np.minimum(large, 31))
    put("onehot", bucket[None] == np.arange(32)[:, None])
    put("rev8", np.tile(8 - np.arange(8), (P, 1)))
    put("steps8", np.tile(SLOTS * np.arange(1, 9), (P, 1)))
    put("iota", np.tile(np.arange(128), (P, 1)))
    put("row32", (p % 32)[:, None])
    put("eps_rms", np.full((P, 1), EPS_RMS))
    put("eps_ln", np.full((P, 1), EPS_LN))
    put("one", np.ones((P, 64)))
    put("blocks", np.tile(np.arange(MORE), (P, 1)))
    put("first", np.tile(SLOTS * np.arange(NE), (P, 1)))
    put("late", np.tile(SLOTS * (NE - 1 - np.arange(NE)), (P, 1)))
    put("groups", np.tile(GROUP * np.arange(MORE // GROUP), (P, 1)))
    return out


class MoeSignals:

    def __init__(self, w13, w2, sel, g_full, xg, up, hs, t, sg, ht, y, ys, put, added, ps, ss):
        self.w13, self.w2, self.sel, self.g_full, self.xg, self.up, self.hs, self.t = w13, w2, sel, g_full, xg, up, hs, t
        self.sg, self.ht, self.y, self.ys, self.put, self.added, self.ps, self.ss = sg, ht, y, ys, put, added, ps, ss


class Steps:

    def __init__(self, eng, own):
        self.eng, self.own, self.sent, self.seen, self.last = eng, own, {}, {}, None

    def done(self, ins, sem=None):
        sem = sem or self.own
        self.sent[sem] = self.sent.get(sem, 0) + 1
        ins.then_inc(sem, 1)
        self.last = (sem, self.sent[sem])

    def settle(self):
        self.eng.wait_ge(*self.last)

    def need(self, sem, k=1):
        self.seen[sem] = self.seen.get(sem, 0) + k
        self.eng.wait_ge(sem, self.seen[sem])


def weight_plan(w):
    plan = []

    def rows(src, a=None, b=None):
        v = src.rearrange("(k p) n -> p k n", p=P)
        return v if a is None else v[:, :, a:b]

    def cols(label, src, ranges):
        def view(buf):
            n = sum(b - a for a, b in ranges)
            v = buf[:, 0:KD * n].rearrange("p (k n) -> p k n", k=KD)
            at, out = 0, []
            for a, b in ranges:
                out.append((v[:, :, at:at + b - a], rows(src, a, b)))
                at += b - a
            return out
        plan.append((label, view))

    def ffn(l, j):
        for g in range(NF // 2):
            def up(buf, g=g):
                v = buf[:, :].rearrange("p (m k n) -> p m k n", m=2, k=KD)
                return [(v[:, 0], rows(w["ffn_w_gate"][l, j], g * 256, g * 256 + 256)),
                        (v[:, 1], rows(w["ffn_w_up"][l, j], g * 256, g * 256 + 256))]
            plan.append((("up", l, j, g), up))
        for c in range(4):
            for h in range(2):
                def down(buf, c=c, h=h):
                    v = buf[:, 0:11 * 256].rearrange("p (k n) -> p k n", k=11)
                    return [(v, rows(w["ffn_w_down"][l, j][h * 11 * P:(h + 1) * 11 * P], c * 256, c * 256 + 256))]
                plan.append((("down", l, j, c, h), down))

    def tall(label, src, kk):
        def view(buf):
            return [(buf[:, 0:kk * D].rearrange("p (k n) -> p k n", k=kk), rows(src))]
        plan.append((label, view))

    for l in range(2):
        ffn(l, 0)
        wi = w["w_in"][l]
        cols(("in3", l), wi, [(C_LF, C_QB), (C_KB, C_GA)])
        cols(("in4", l), wi, [(C_QB, C_KB)])
        cols(("in0", l), wi, [(C_QA, C_VA)])
        cols(("in1", l), wi, [(C_VA, C_RA)])
        cols(("in2", l), wi, [(C_RA, C_LF)])
        for c in range(4):
            cols(("gate", l, c), wi, [(C_GA + 512 * c, C_GA + 512 * c + 512)])
        tall(("pa", l), w["w_pa"][l], 4)
        tall(("pb", l), w["w_pb"][l], 4)
        for c in range(2):
            cols(("out", l, c), w["w_out"][l], [(512 * c, 512 * c + 512)])
        ffn(l, 1)
    for k in range(KD):
        cols(("conv", k), w["conv_w_in_2"][0], [(q * D + k * P, q * D + k * P + P) for q in range(3)])
    for c in range(2):
        cols(("convout", c), w["conv_w_out_2"][0], [(512 * c, 512 * c + 512)])
    plan.append((("moe", 0), None))
    wi = w["attn_w_in_2"][0]
    cols(("d_idx",), wi, [(C_CKV, C_QI), (C_KI, C_END2)])
    cols(("d_qi",), wi, [(C_QI, C_KI)])
    for c in range(4):
        cols(("d_q", c), wi, [(512 * c, 512 * c + 512)])
    for c in range(4):
        def view(buf, c=c):
            v = buf[:, :].rearrange("p (k n) -> p k n", k=NH2)
            return [(v, rows(w["attn_w_out_2"][0], 256 * c, 256 * c + 256))]
        plan.append((("d_out", c), view))
    plan.append((("moe", 1), None))
    return plan


ARENA_N = 24300


def build_model(nc, w, cst_dram, small_dram, h0_dram, table_dram, out_dram):
    CL, SL = const_layout(), small_layout()
    with ExitStack() as ctx:
        def sb(name, shape, dt=F32):
            return ctx.enter_context(nc.sbuf_tensor(name, shape, dt))

        def sem(name):
            return ctx.enter_context(nc.semaphore(name))

        CST, SM = sb("CST", [P, CL.n]), sb("SM", [P, SL.n])
        H = sb("H", [P, KD, T])
        XN = sb("XN", [P, KD, T])
        SQ = sb("SQ", [P, KD, T])
        RS = sb("RS", [P, T])
        RW = sb("RW", [P, KD, 72])
        IDS = sb("IDS", [1, MORE + 1], I32)
        RING_B = [sb(f"wring{i}", [P, SLOT]) for i in range(RING)]
        ARENA = sb("ARENA", [P, ARENA_N])
        bank = [ctx.enter_context(nc.psum_tensor(f"bank{i}", [P, 512], F32)) for i in range(8)]
        X2, R2 = H[:, :, 0:SEQ], XN[:, :, 0:SEQ]

        def const(name, rows=P):
            return CL(CST, name, rows)

        def small(name, rows=P):
            return SL(SM, name, rows)

        class Arena:

            def __init__(self, start=0):
                self.n = start

            def __call__(self, *shape):
                n = int(np.prod(shape))
                v = ARENA[:, self.n:self.n + n]
                self.n += n
                assert self.n <= ARENA_N, self.n
                names = "abcd"[:len(shape)]
                kw = {names[i]: shape[i] for i in range(1, len(shape))}
                return v.rearrange(f"p ({' '.join(names)}) -> p {' '.join(names)}", **kw) if kw else v

        bank_full = {e: [sem(f"bank{b}_full_{e}") for b in range(8)] for e in ("act", "dve")}
        bank_free = {e: [sem(f"bank{b}_free_{e}") for b in range(8)] for e in ("act", "dve")}
        act_step, dve_step = sem("act_step"), sem("dve_step")
        w_ready = [sem(f"w_ready{i}") for i in range(RING)]
        half_used = sem("down_half_used")
        x_at = {}
        loaded = sem("loaded")
        rw_ready = sem("router_weights_ready")
        h_tile = sem("h_tile")
        sum_tile = sem("sum_tile")
        x_tile = sem("x_tile")
        sq_ready = sem("sq_ready")
        std_ready = sem("std_ready")
        xn_ready = sem("xn_ready")
        silu_ready = sem("silu_ready")
        hid_ready = sem("hid_ready")
        a2d, a2p = sem("act_result_for_dve"), sem("act_result_for_pe")
        d2a, d2p = sem("dve_result_for_act"), sem("dve_result_for_pe")
        rows_done = sem("products_from_other_rows_done")
        pv_done = sem("values_product_done")
        gla_ready = sem("decayed_keys_ready")
        tbl_row, tbl_w, tbl_r = sem("bias_row_ready"), sem("bias_table_written"), sem("bias_table_read")
        ids_ready = sem("ids_ready")
        M = []
        for l in range(2):
            M.append(MoeSignals(
                w13=[sem(f"moe{l}_w13_ready{i}") for i in range(GROUP)],
                w2=[sem(f"moe{l}_w2_ready{i}") for i in range(GROUP)],
                **{k: sem(f"moe{l}_{name}") for k, name in (
                    ("sel", "select_ready"), ("g_full", "gather_full"), ("xg", "gathered"), ("up", "up_full"),
                    ("hs", "up_copied"), ("t", "turned"), ("sg", "silu_ready"), ("ht", "hidden_ready"),
                    ("y", "down_full"), ("ys", "down_copied"), ("put", "put_ready"), ("added", "added"),
                    ("ps", "put_step"), ("ss", "select_step"))}))
        stored = sem("stored")

        plan = weight_plan(w)
        where, count, owner, n = {}, [0] * RING, [None] * RING, 0
        for label, view in plan:
            if view is None:
                where[label] = (0, 0, list(owner))
                n, owner = 0, [None] * RING
                continue
            s = n % RING
            n += 1
            count[s] += 16 * len(view(RING_B[s]))
            where[label] = (s, count[s], owner[s])
            owner[s] = label
        last_use = {}

        a = Arena()
        HID, SG = a(NF, T), a(2, T)
        BROW, BBUF = a(NH2, 384), a(NH2, 384)
        a = Arena()
        QK, VA, RA, LR, VB = a(4, T), a(3, 512), a(4, T), a(T), a(3, 128)
        QR, GA, GB, BT, AT = a(6, T), a(KD, T), a(KD, T), a(4, T), a(4, T)
        PR, PT, ST1 = a(2, T), a(2, 3, 128), a(8, 4)
        GT, BC, EL = a(4, T), a(4, T), a(4, T)
        QB, XR = Arena(a.n)(6, T), Arena(a.n + 6 * T)(6, T)
        QD, KI, KE = a(2, 2, T), a(2, 2, T), a(2, 2, T)
        KET = SQ[:, 0:6, :].rearrange("p a b -> p (a b)")[:, 0:1536].rearrange("p (a b c) -> p a b c", a=3, b=2)
        ST = a(2, 4, 256)
        ATT, ATM, DEC = a(2, 8, 64), a(2, 64), a(4, 4)
        S2 = SQ[:, 0:6, :]
        a = Arena()
        CV_C, CV_U, CV_T, CV_V = a(2, SEQ), a(2, SEQ + 2), a(2, SEQ), a(KD, SEQ)
        a = Arena()
        CK, CKN, CKT, KX, KN2, WI = a(SEQ), a(SEQ), a(2, P), a(SEQ), a(SEQ), a(2, 8)
        QI, Q2, O2 = a(4, SEQ), a(NH2, SEQ), a(NH2, SEQ)
        SC, WK, MSK = a(2, SEQ), a(2, SEQ), a(2, SEQ)
        BIAS0, BIAS1 = a(NH2, P), a(NH2, SEQ)
        RL, LG2, PR2, PT2, M8, ST2 = a(2, SEQ), a(2, SEQ), a(2, SEQ), a(2, 2, P), a(8), a(8, 4)
        a = Arena()
        XTOK, XG, HS, YS, SGM, HT, PUT, PUT2 = a(2, D), a(KD, P), a(512), a(512), a(64), a(64), a(2, SEQ), a(SEQ)
        LG, E8, G8, OHG, ES, OH = a(2, 72), a(2, 8), a(8, 2), a(2, 8), a(2, 8), a(2, 2, 8)
        TMP, MA, RK, CMP, CNT, SLT = a(2, 64), a(3, 2, 64), a(2, 64), a(64, 8), a(5, 64), a(8, 2)
        DG, ROWS, GS, PC, SLC, CMB = a(8, P), a(4, SEQ), a(2, P), a(GROUP), a(4), a(MORE)
        YT, SCR8 = a(2, D), a(2, 8)
        W2B = a(GROUP, 2048)

        block = ctx.enter_context(nc.Block())

        def atleast(eng, s, value):
            if not isinstance(value, int) or value > 0:
                eng.wait_ge(s, value)

        def own_and_more(eng, l, group):
            with eng.Fori(1, NG0) as i:
                group(i)
            eng.wait_ge(ids_ready, l + 1)
            n = NG0 + eng.value_load(IDS[0:1, MORE:MORE + 1], min_val=0, max_val=NG - NG0)
            with eng.Fori(NG0, NG) as i:
                with eng.If(i < n):
                    group(i)
            return n
        @block.tensor
        def _(pe):
            st = Steps(pe, None)
            held = {}

            def claim(b):
                if b in held:
                    st.need(bank_free[held.pop(b)][b])

            def products(b, reader, freer, groups):
                claim(b)
                for g in groups:
                    if g is None:
                        st.done(ins, rows_done)
                        st.settle()
                        continue
                    for i, (o, l, r) in enumerate(g):
                        ins = nc.tensor.matmul(o, l, r, start=(i == 0), stop=(i == len(g) - 1))
                st.done(ins, bank_full[reader][b])
                if freer:
                    held[b] = freer

            def turns(b, reader, freer, items):
                claim(b)
                for o, i in items:
                    n = i.shape[0]
                    ins = nc.tensor.transpose(o, i, const("ident", n)[:, 0:n])
                st.done(ins, bank_full[reader][b])
                if freer:
                    held[b] = freer

            def slot(label):
                s, ready, _ = where[label]
                pe.wait_ge(w_ready[s], ready)
                return RING_B[s]

            def used(label):
                last_use[label] = st.last

            def cols_of(label, n):
                return slot(label)[:, 0:KD * n].rearrange("p (k n) -> p k n", k=KD)

            def rows(x, n=T):
                return [x[:, k, 0:n] for k in range(KD)]

            def column_means(b, wgt, tiles, reader):
                claim(b)
                for k, x in enumerate(tiles):
                    st.need(sq_ready)
                    ins = nc.tensor.matmul(bank[b][:, 0:x.shape[1]], const(wgt), x, start=(k == 0),
                                           stop=(k == len(tiles) - 1))
                st.done(ins, bank_full[reader][b])

            def rms_norm():
                column_means(7, "mean_d", rows(SQ), "act")

            def layer_norm(b):
                claim(b)
                for k in range(KD):
                    st.need(sum_tile)
                    ins = nc.tensor.matmul(bank[b][:, 0:SEQ], const("mean_d"), R2[:, k, :], start=(k == 0),
                                           stop=(k == KD - 1))
                st.done(ins, bank_full["dve"][b])
                held[b] = "dve"
                column_means(b + 1, "mean_d", rows(SQ, SEQ), "act")
                st.need(x_tile, KD)

            def ffn(l, j):
                rms_norm()
                for g in range(NF // 2):
                    v = slot(("up", l, j, g))[:, :].rearrange("p (m k n) -> p m k n", m=2, k=KD)
                    for ft in range(2):
                        pair = 2 * ((2 * g + ft) % 2)
                        if 2 * g + ft >= 2:
                            st.need(hid_ready)
                        for m, e in ((0, "act"), (1, "dve")):
                            claim(pair + m)
                            for k in range(KD):
                                if g == 0 and ft == 0 and m == 0:
                                    st.need(xn_ready)
                                ins = nc.tensor.matmul(bank[pair + m][:, 0:T], v[:, m, k, ft * P:(ft + 1) * P],
                                                       XN[:, k, :], start=(k == 0), stop=(k == KD - 1))
                            st.done(ins, bank_full[e][pair + m])
                    used(("up", l, j, g))
                for c in range(4):
                    for h in range(2):
                        v = slot(("down", l, j, c, h))[:, 0:11 * 256].rearrange("p (k n) -> p k n", k=11)
                        for dt in range(2):
                            b = (4 if c % 2 == 0 else 0) + dt
                            if h == 0:
                                claim(b)
                            for f in range(11):
                                if c == 0 and dt == 0 and h * 11 + f >= NF - 2:
                                    st.need(hid_ready)
                                ins = nc.tensor.matmul(bank[b][:, 0:T], v[:, f, dt * P:(dt + 1) * P],
                                                       HID[:, h * 11 + f, :], start=(h == 0 and f == 0),
                                                       stop=(h == 1 and f == 10))
                            if h == 1:
                                st.done(ins, bank_full["dve"][b])
                                held[b] = "dve"
                            elif dt == 1:
                                st.done(ins, half_used)
                        used(("down", l, j, c, h))

            def gate_block(l, c):
                v = cols_of(("gate", l, c), 512)
                for m in range(4):
                    products(6 + m % 2, "act", "act",
                             [[(bank[6 + m % 2][:, 0:T], v[:, k, m * P:(m + 1) * P], x) for k, x in enumerate(rows(XN))]])
                used(("gate", l, c))

            def mixer(l):
                rms_norm()
                st.need(xn_ready, KD)
                v = cols_of(("in3", l), 288)
                products(0, "dve", "dve",
                         [[(bank[0][32 * d:32 * d + 16, 0:T], v[:, k, 16 * d:16 * d + 16], x)
                           for k, x in enumerate(rows(XN))] for d in range(2)])
                for kv in range(2):
                    products(1 + kv, "act", "dve",
                             [[(bank[1 + kv][64 * half:64 * half + 64, 0:T], v[:, k, 32 + 64 * kv:96 + 64 * kv], x)
                               for k, x in enumerate(rows(XN))] for half in range(2)])
                products(3, "act", "act",
                         [[(bank[3][0:nt, t * P:(t + 1) * P], XN[:, k, a:a + nt], v[:, k, 160:288])
                           for k in range(KD)] for t, (a, nt) in enumerate(TILES)])
                used(("in3", l))
                v = cols_of(("in4", l), 512)
                for m in range(4):
                    products(4 + m, "act", "dve",
                             [[(bank[4 + m][:, 0:T], v[:, k, m * P:(m + 1) * P], x) for k, x in enumerate(rows(XN))]])
                used(("in4", l))
                v = cols_of(("in0", l), 512)
                for m in range(4):
                    products(m, "act", "act",
                             [[(bank[m][:, 0:T], v[:, k, m * P:(m + 1) * P], x) for k, x in enumerate(rows(XN))]])
                used(("in0", l))
                for i in range(4):
                    d, tile = i // 2, i % 2
                    products(4 + i, "dve", "dve",
                             [[(bank[4 + i][:, 0:T],
                                small("gla_w")[32 * d:32 * d + 16, l * 256 + tile * P:l * 256 + tile * P + P],
                                LR[32 * d:32 * d + 16, :])]])
                for i in range(6):
                    products(i, "act", None, [[(bank[i][:, 0:T], const("mean64"), S2[:, i, :])]])
                v = cols_of(("in1", l), 512)
                for t, (a_, nt) in enumerate(TILES):
                    b = (6, 7, 6)[t]
                    products(b, "act", "act",
                             [[(bank[b][0:nt, :], XN[:, k, a_:a_ + nt], v[:, k, :]) for k in range(KD)]])
                used(("in1", l))
                for i in range(6):
                    st.need(d2p)
                    products(i, "dve", "dve", [[(bank[i][:, 0:T], const("swap"), XR[:, i, :])]])
                v = cols_of(("in2", l), 512)
                for m in range(4):
                    b = (6, 7)[m % 2]
                    products(b, "act", "act",
                             [[(bank[b][:, 0:T], v[:, k, m * P:(m + 1) * P], x) for k, x in enumerate(rows(XN))]])
                used(("in2", l))
                st.need(d2p)
                units = [(h, t) for h in range(8) for t in range(3)]

                def scores(n):
                    h, t = units[n]
                    a_, nt = TILES[t]
                    hp = 64 * (h % 2)
                    products(n % 2, "dve", "dve",
                             [[(bank[n % 2][0:nt, 0:T], QR[hp:hp + 64, h // 2, a_:a_ + nt],
                                QR[hp:hp + 64, 4 + h // 4, :])]])

                def turn_rows(n):
                    h, t = units[n]
                    nt = TILES[t][1]
                    st.need(d2p)
                    turns(2 + n % 2, "dve", None,
                          [(bank[2 + n % 2][0:nk, kt * P:kt * P + nt], PR[0:nt, n % 2, c:c + nk])
                           for kt, (c, nk) in enumerate(TILES)])

                def values(n):
                    h, t = units[n]
                    a_, nt = TILES[t]
                    st.need(d2p)
                    hp, b = 64 * (h % 2), 4 + h // 2 % 2
                    if t == 0 and h % 2 == 0:
                        claim(b)
                    for kt, (c, nk) in enumerate(TILES):
                        ins = nc.tensor.matmul(bank[b][hp:hp + 64, a_:a_ + nt],
                                               VB[0:nk, kt, 64 * (h // 4):64 * (h // 4) + 64],
                                               PT[0:nk, n % 2, kt, 0:nt], start=(kt == 0), stop=(kt == 2))
                    if t == 2 and h % 2 == 1:
                        st.done(ins, bank_full["act"][b])
                        held[b] = "act"
                    else:
                        st.done(ins, pv_done)

                for n in range(len(units) + 2):
                    if n < len(units):
                        scores(n)
                    if 1 <= n <= len(units):
                        turn_rows(n - 1)
                    if n >= 2:
                        values(n - 2)
                    if n % 6 == 5:
                        gate_block(l, n // 6)
                st.need(gla_ready)
                for t, (c, nt) in enumerate(TILES):
                    turns(t, "dve", "dve",
                          [(bank[t][0:nt, i * P:(i + 1) * P], KE[:, i // 2, i % 2, c:c + nt]) for i in range(4)])
                for d in range(2):
                    g = []
                    for h in (0, 2, 1, 3):
                        hp = 64 * (h % 2)
                        if h == 1:
                            g.append(None)
                        for t in range(2):
                            for c in range(2):
                                at = t * P + c * 64
                                g.append([(bank[3 + d][64 * c:64 * c + 64, (2 * h + t) * 64:(2 * h + t) * 64 + 64],
                                           KI[hp:hp + 64, d, h // 2, at:at + 64], QD[hp:hp + 64, d, h // 2, at:at + 64])])
                    products(3 + d, "dve", "dve", g)
                def meta_scores(d, h):
                    return [(bank[5][0:META, d * 64 + h * META:d * 64 + h * META + META],
                             KI[64 * (h % 2):64 * (h % 2) + 64, d, h // 2, SEQ:T],
                             QD[64 * (h % 2):64 * (h % 2) + 64, d, h // 2, SEQ:T])]

                products(5, "dve", "dve", [meta_scores(d, h) for d in range(2) for h in (0, 2)] + [None]
                         + [meta_scores(d, h) for d in range(2) for h in (1, 3)])
                for b in range(3):
                    claim(b)
                for d, steps in ((0, (4, 0, 1, 2)), (1, (3, 2, 1, 0))):
                    for half in range(2):
                        b = 6 + half if d == 0 else half
                        g = []
                        for q in range(2):
                            c = steps[2 * half + q]
                            r0, nr, t = (0, META, 2) if c == 4 else (64 * (c % 2), 64, c // 2)
                            if q == 1:
                                g.append(None)
                            for h in range(4):
                                g.append([(bank[b][64 * (h % 2):64 * (h % 2) + 64,
                                                   q * 256 + h // 2 * P:q * 256 + h // 2 * P + P],
                                           KET[r0:r0 + nr, t, d, h * 64:h * 64 + 64],
                                           VA[r0:r0 + nr, t, h * P:h * P + P])])
                        products(b, "dve", "dve", g)
                for b in (3, 4, 5, 6, 7, 0, 1):
                    claim(b)
                for h in range(4):
                    hp, by_row = 64 * (h % 2), {0: [], 64: []}
                    tile = slice(h // 2 * P, h // 2 * P + P)
                    for c in range(4):
                        r0, t, at = 64 * (c % 2), c // 2, c * 64
                        o = bank[2 + h][:, at:at + 64]
                        for d in range(2):
                            by_row[r0].append((o, VA[r0:r0 + 64, t, h * P:h * P + P], ATT[r0:r0 + 64, d, 2 * h + t, :]))
                        by_row[hp].append((o, ST[hp:hp + 64, 0, c, tile], QD[hp:hp + 64, 0, h // 2, at:at + 64]))
                        if c < 3:
                            by_row[hp].append((o, ST[hp:hp + 64, 1, 2 - c, tile], QD[hp:hp + 64, 1, h // 2, at:at + 64]))
                    o = bank[2 + h][:, SEQ:T]
                    for d in range(2):
                        by_row[0].append((o, VA[0:META, 2, h * P:h * P + P], ATM[0:META, d, h * META:h * META + META]))
                    by_row[hp].append((o, ST[hp:hp + 64, 1, 3, tile], QD[hp:hp + 64, 1, h // 2, SEQ:T]))
                    claim(2 + h)
                    for r0 in (0, 64):
                        for i, (o, l_, r_) in enumerate(by_row[r0]):
                            ins = nc.tensor.matmul(o, l_, r_, start=(r0 == 0 and i == 0),
                                                   stop=(r0 == 64 and i == len(by_row[64]) - 1), skip_group_check=True)
                        if r0 == 0:
                            st.done(ins, rows_done)
                            st.settle()
                    st.done(ins, bank_full["act"][2 + h])
                    held[2 + h] = "dve"
                for h in range(4):
                    b = (0, 1, 6, 7)[h]
                    st.need(sq_ready)
                    products(b, "act", None, [[(bank[b][:, 0:T], const("mean128"), SQ[:, h, :])]])
                va = slot(("pa", l))[:, :].rearrange("p (k n) -> p k n", k=4)
                vb = slot(("pb", l))[:, :].rearrange("p (k n) -> p k n", k=4)
                st.need(d2p)
                for k in range(KD):
                    for m, (v, x) in enumerate(((va, AT), (vb, BT))):
                        b = 2 * (k % 2) + m
                        products(b, "dve", "dve",
                                 [[(bank[b][:, 0:T], v[:, q, k * P:(k + 1) * P], x[:, q, :]) for q in range(4)]])
                        used(("pa" if m == 0 else "pb", l))
                st.need(d2p)
                for c in range(2):
                    v = cols_of(("out", l, c), 512)
                    for m in range(4):
                        b = 4 + m
                        products(b, "dve", "dve",
                                 [[(bank[b][:, 0:T], v[:, k, m * P:(m + 1) * P], x) for k, x in enumerate(rows(GA))]])
                    used(("out", l, c))

            def bias_rows():
                for h in range(NH2):
                    st.need(d2p)
                    products(h % 2, "act", "act",
                             [[(bank[h % 2][:, 0:384], const("ones", 32), BROW[0:32, h, :])]])

            def convolution():
                st.need(x_tile, KD)
                for k in range(KD):
                    v = cols_of(("conv", k), 384)
                    for q, e in ((1, "act"), (2, "dve"), (0, "dve")):
                        b = 3 * (k % 2) + q
                        products(b, e, e, [[(bank[b][:, 0:SEQ], v[:, kk, q * P:(q + 1) * P], x)
                                            for kk, x in enumerate(rows(X2, SEQ))]])
                    used(("conv", k))
                st.need(d2p, KD)
                for c in range(2):
                    v = cols_of(("convout", c), 512)
                    for m in range(4):
                        b = (6, 7)[m % 2]
                        products(b, "dve", "dve",
                                 [[(bank[b][:, 0:SEQ], v[:, kk, m * P:(m + 1) * P], x)
                                   for kk, x in enumerate(rows(CV_V, SEQ))]])
                    used(("convout", c))

            def attention():
                v = cols_of(("d_idx",), 200)
                xs = rows(X2, SEQ)
                products(0, "dve", "dve", [[(bank[0][:, 0:SEQ], v[:, k, 0:P], x) for k, x in enumerate(xs)]])
                products(1, "dve", "dve",
                         [[(bank[1][64 * half:64 * half + 64, 0:SEQ], v[:, k, P:P + 64], x)
                           for k, x in enumerate(xs)] for half in range(2)])
                products(2, "dve", "dve",
                         [[(bank[2][:, 8 * t:8 * t + 8], X2[:, k, t * P:(t + 1) * P], v[:, k, 192:200])
                           for k in range(KD)] for t in range(2)])
                used(("d_idx",))
                v = cols_of(("d_qi",), 512)
                for m in range(4):
                    products(3 + m, "act", "act",
                             [[(bank[3 + m][:, 0:SEQ], v[:, k, m * P:(m + 1) * P], x) for k, x in enumerate(xs)]])
                used(("d_qi",))
                st.need(d2p)
                products(7, "dve", "dve", [[(bank[7][:, 0:SEQ], const("mean64"), KX)]])
                st.need(a2p)
                products(0, "act", None, [[(bank[0][:, 0:SEQ], const("mean128"), SQ[:, 0, 0:SEQ])]])
                st.need(a2p)
                products(1, "act", None, [[(bank[1][:, 0:SEQ], const("mean64"), SQ[:, 1, 0:SEQ])]])
                st.need(d2p)
                turns(2, "act", "act", [(bank[2][:, t * P:(t + 1) * P], CKN[:, t * P:(t + 1) * P]) for t in range(2)])
                for c in range(2):
                    v = cols_of(("d_q", c), 512)
                    for m in range(4):
                        products(3 + m, "act", "act",
                                 [[(bank[3 + m][:, 0:SEQ], v[:, k, m * P:(m + 1) * P], x) for k, x in enumerate(xs)]])
                    used(("d_q", c))
                st.need(d2p)
                for n in range(16):
                    t, h = n // 8, n % 8
                    hp = 64 * (h % 2)
                    products(n % 2, "act", "dve",
                             [[(bank[n % 2][:, 0:P * (t + 1)], QI[hp:hp + 64, h // 2, t * P:(t + 1) * P],
                                KN2[hp:hp + 64, 0:P * (t + 1)])]])
                for c in range(2, 4):
                    v = cols_of(("d_q", c), 512)
                    for m in range(4):
                        products(3 + m, "act", "act",
                                 [[(bank[3 + m][:, 0:SEQ], v[:, k, m * P:(m + 1) * P], x) for k, x in enumerate(xs)]])
                    used(("d_q", c))
                for b in range(2, 7):
                    claim(b)
                units = [(h, t) for h in range(NH2) for t in range(2)]

                def scores(n):
                    h, t = units[n]
                    products(n % 2, "dve", "dve",
                             [[(bank[n % 2][:, 0:P * (t + 1)], Q2[:, h, t * P:(t + 1) * P], CKN[:, 0:P * (t + 1)])]])

                def turn_rows(n):
                    h, t = units[n]
                    st.need(d2p)
                    turns(2 + n % 2, "act", None,
                          [(bank[2 + n % 2][:, s * P:(s + 1) * P], PR2[:, n % 2, s * P:(s + 1) * P])
                           for s in range(t + 1)])

                def values(n):
                    h, t = units[n]
                    st.need(a2p)
                    b = 4 + h % 2
                    if t == 0:
                        claim(b)
                    for s in range(t + 1):
                        ins = nc.tensor.matmul(bank[b][:, t * P:(t + 1) * P], CKT[:, s, :], PT2[:, n % 2, s, :],
                                               start=(s == 0), stop=(s == t))
                    if t == 1:
                        st.done(ins, bank_full["act"][b])
                        held[b] = "act"
                    else:
                        st.done(ins, pv_done)

                for n in range(len(units) + 2):
                    if n < len(units):
                        scores(n)
                    if 1 <= n <= len(units):
                        turn_rows(n - 1)
                    if n >= 2:
                        values(n - 2)
                for b in (4, 5):
                    claim(b)
                for c in range(4):
                    v = slot(("d_out", c))[:, :].rearrange("p (k n) -> p k n", k=NH2)
                    for m in range(2):
                        b = 6 + m
                        products(b, "dve", "dve",
                                 [[(bank[b][:, 0:SEQ], v[:, q, m * P:(m + 1) * P], O2[:, q, :]) for q in range(NH2)]])
                    used(("d_out", c))

            def experts(l):
                pe.wait_ge(rw_ready, 32 * (l + 1))
                products(0, "dve", "dve",
                         [[(bank[0][:, t * 72:(t + 1) * 72], X2[:, k, t * P:(t + 1) * P], RW[:, k, :])
                           for k in range(KD)] for t in range(2)])
                for q in range(4):
                    turns(4 + q, "act", "act",
                          [(bank[4 + q][:, kk * P:(kk + 1) * P],
                            X2[:, (q % 2) * 4 + kk, q // 2 * P:(q // 2 + 1) * P]) for kk in range(4)])
                st.need(d2p)
                B = bank[1]
                products(1, "dve", "dve",
                         [[(B[:, 0:64], const("before"), MA[:, 2, 0, :])],
                          [(B[:, 64:128], const("ones"), MA[:, 2, 0, :]), (B[:, 64:128], const("before"), MA[:, 2, 1, :])],
                          [(B[:, 128:192], const("ones"), MA[:, 2, 0, :]), (B[:, 128:192], const("ones"), MA[:, 2, 1, :])]])
                st.need(d2p)
                products(2, "dve", "dve", [[(bank[2][:, 0:MORE], const("ones", 64), CMB[0:64, :])]])
                st.need(d2p)
                for q in range(2):
                    products((3, 0)[q], "act", "act",
                             [[(bank[(3, 0)[q]][:, i * P:(i + 1) * P], const("ones"), DG[:, 4 * q + i, :])]
                              for i in range(4)])
                for b in list(held):
                    claim(b)
                UP, TURN, DOWN, GATHER = bank[4], bank[5], bank[6], bank[7]
                m = M[l]

                def gather(i):
                    pe.wait_ge(m.sel, i + 1)
                    for half in range(2):
                        atleast(pe, m.xg, 2 * i + half)
                        for kk in range(4):
                            k = 4 * half + kk
                            for t in range(2):
                                ins = nc.tensor.matmul(GATHER[:, kk * P:(kk + 1) * P], XTOK[:, t, k * P:(k + 1) * P],
                                                       GS[:, t, :], start=(t == 0), stop=(t == 1))
                        ins.then_inc(m.g_full, 1)
                    pe.wait_ge(m.xg, 2 * i + 2)

                def down(b, u, i):
                    pe.wait_ge(m.ht, b + 1)
                    pe.wait_ge(m.w2[u], 16 * (i + 1))
                    atleast(pe, m.ys, b)
                    w2 = W2B[:, u, :].rearrange("p (k n) -> p k n", k=2)
                    for q in range(4):
                        dh, c = q // 2, q % 2
                        ins = nc.tensor.matmul(DOWN[32 * q:32 * q + 32, :], HT[:, c * 32:c * 32 + 32],
                                               w2[:, c, dh * 512:dh * 512 + 512], start=True, stop=True,
                                               tile_position=(0, 32 * q))
                    ins.then_inc(m.y, 1)

                def put(b, u, first, last):
                    pe.wait_ge(m.ys, b + 1)
                    pe.wait_ge(m.put, b + 1)
                    for t in range(2):
                        for dh in range(2):
                            ins = nc.tensor.matmul(bank[2 * t + dh][:, :], PUT[64 * dh:64 * dh + 64, u % 2, t * P:(t + 1) * P],
                                                   YS[64 * dh:64 * dh + 64, :], start=first, stop=last,
                                                   skip_group_check=True)
                    ins.then_inc(m.added, 1)

                def group(i):
                    peeled = isinstance(i, int)
                    gather(i)
                    for u in range(GROUP):
                        b = GROUP * i + u
                        pe.wait_ge(m.w13[u], 32 * (i + 1))
                        atleast(pe, m.hs, b)
                        v = RING_B[u][:, :].rearrange("p (k n) -> p k n", k=KD)
                        for k in range(KD):
                            q = k % 4
                            ins = nc.tensor.matmul(UP[32 * q:32 * q + 32, :], XG[:, k, u * 32:u * 32 + 32], v[:, k, :],
                                                   start=(k < 4), stop=(k >= 4), tile_position=(0, 32 * q))
                        ins.then_inc(m.up, 1)
                        if not (peeled and u == 0):
                            down(b - 1, (u - 1) % GROUP, i if u else i - 1)
                        pe.wait_ge(m.hs, b + 1)
                        atleast(pe, m.ht, b)
                        for f in range(4):
                            ins = nc.tensor.matmul(TURN[:, f * 32:f * 32 + 32], HS[:, f * P:(f + 1) * P], const("sum4"),
                                                   start=True, stop=True)
                        ins.then_inc(m.t, 1)
                        if not (peeled and u == 0):
                            put(b - 1, (u - 1) % GROUP, peeled and u == 1, False)

                group(0)
                n = own_and_more(pe, l, group)
                down(GROUP * n - 1, GROUP - 1, n - 1)
                pe.wait_ge(m.ys, GROUP * n)
                pe.wait_ge(m.put, GROUP * n)
                for b in range(4):
                    t, dh = b // 2, b % 2
                    ins = nc.tensor.matmul(bank[b][:, :], PUT[64 * dh:64 * dh + 64, (GROUP - 1) % 2, t * P:(t + 1) * P],
                                           YS[64 * dh:64 * dh + 64, :], start=False, stop=True, skip_group_check=True)
                    st.done(ins, bank_full["act"][b])
                    held[b] = "act"
                for b in range(4):
                    claim(b)
                for k in range(KD):
                    turns(4 + k % 4, "dve", "dve",
                          [(bank[4 + k % 4][:, t * P:(t + 1) * P], YT[:, t, k * P:(k + 1) * P]) for t in range(2)])

            pe.wait_ge(loaded, 48)
            bias_rows()
            for l in range(2):
                ffn(l, 0)
                mixer(l)
                ffn(l, 1)
            rms_norm()
            convolution()
            layer_norm(0)
            experts(0)
            layer_norm(0)
            attention()
            layer_norm(4)
            experts(1)
            layer_norm(0)

        @block.scalar
        def _(act):
            st = Steps(act, act_step)
            A = nc.scalar.activation

            def mark(s):
                st.settle()
                st.done(act.nop(), s)

            def copy(out, b, view, s=None):
                st.need(bank_full["act"][b])
                st.done(A(out, view, ACT.Copy), s or bank_free["act"][b])

            def squares(first=False):
                for k in range(KD):
                    if not first:
                        st.need(h_tile)
                    st.done(A(SQ[:, k, :], H[:, k, :], ACT.Square), sq_ready)

            def deviation(out, b, eps, n, s):
                st.need(bank_full["act"][b])
                st.done(A(out, bank[b][:, 0:n], ACT.Sqrt, bias=const(eps)), s)

            def rms_norm(first=False):
                squares(first)
                deviation(RS[:, :], 7, "eps_rms", T, std_ready)

            def layer_norm(b):
                st.need(d2a)
                for k in range(KD):
                    st.done(A(SQ[:, k, 0:SEQ], R2[:, k, :], ACT.Square), sq_ready)
                deviation(RS[:, 0:SEQ], b + 1, "eps_ln", SEQ, std_ready)

            def ffn(first=False):
                rms_norm(first)
                for f in range(NF):
                    pair = 2 * (f % 2)
                    if f >= 2:
                        st.need(hid_ready)
                    st.need(bank_full["act"][pair])
                    st.done(A(SG[:, f % 2, :], bank[pair][:, 0:T], ACT.Silu), silu_ready)
                st.need(hid_ready, 2)

            def gate_block(l, c):
                for m in range(4):
                    b, g = 6 + m % 2, c * 4 + m
                    dst = (GA, GB)[g // 8][:, g % 8, :]
                    st.need(bank_full["act"][b])
                    at = l * 16 + g
                    st.done(A(dst, bank[b][:, 0:T], ACT.Sigmoid, bias=small("bmerge")[:, at:at + 1]),
                            bank_free["act"][b])

            def mixer(l):
                rms_norm()
                if l == 0:
                    act.wait_ge(tbl_w, 16)
                for i, b in ((4, 1), (5, 2)):
                    st.need(bank_full["act"][b])
                    st.done(A(S2[:, i, :], bank[b][:, 0:T], ACT.Square), a2d)
                st.need(bank_full["act"][3])
                st.done(A(VB[:, 0:2, :], bank[3][:, 0:256].rearrange("p (a b) -> p a b", a=2), ACT.Copy))
                st.done(A(VB[0:META, 2, :], bank[3][0:META, 256:384], ACT.Copy), bank_free["act"][3])
                for i in range(4):
                    st.need(bank_full["act"][4 + i])
                    st.done(A(S2[:, i, :], bank[4 + i][:, 0:T], ACT.Square), a2d)
                for m in range(4):
                    copy(QK[:, m, :], m, bank[m][:, 0:T])
                for i in range(6):
                    deviation(S2[:, i, :], i, "eps_rms", T, a2d)
                for t, (a_, nt) in enumerate(TILES):
                    b = (6, 7, 6)[t]
                    copy(VA[0:nt, t, :], b, bank[b][0:nt, :])
                st.need(d2a)
                st.done(A(EL, GT, ACT.Abs))
                st.settle()
                st.done(A(EL, EL, ACT.Exp, scale=-1.0))
                st.settle()
                st.done(A(EL, EL, ACT.Ln, bias=const("one")[:, 0:1]), a2d)
                for m in range(4):
                    b = (6, 7)[m % 2]
                    st.need(bank_full["act"][b])
                    st.done(A(RA[:, m, :], bank[b][:, 0:T], ACT.Silu), bank_free["act"][b])
                st.need(d2a)
                A(QD[:, 0], BC[:, 0:2, :], ACT.Exp)
                A(KI[:, 0], BC[:, 0:2, :], ACT.Exp, scale=-1.0)
                A(QD[:, 1], GT[:, 2:4, :], ACT.Exp)
                A(KI[:, 1], GT[:, 2:4, :], ACT.Exp, scale=-1.0)
                A(KE[:, 0], EL[:, 0:2, :], ACT.Exp)
                A(KE[:, 1], KE[:, 1], ACT.Exp)
                st.done(A(DEC, BC[:, :, 63:256:64], ACT.Exp), a2d)
                units = [(h, t) for h in range(8) for t in range(3)]
                for n in range(len(units) + 2):
                    if n < len(units):
                        h, t = units[n]
                        nt = TILES[t][1]
                        st.need(d2a)
                        st.done(A(PR[0:nt, n % 2, :], bank[n % 2][0:nt, 0:T], ACT.Exp,
                                  bias=ST1[0:nt, n % 8, 0:1], accum_out=ST1[0:nt, n % 8, 1:2]), a2d)
                    if n >= 2 and units[n - 2][1] == 2 and units[n - 2][0] % 2 == 1:
                        hp = units[n - 2][0] // 2
                        copy(BT[:, hp, :], 4 + hp % 2, bank[4 + hp % 2][:, 0:T])
                    if n % 6 == 5:
                        gate_block(l, n // 6)
                for h in range(4):
                    st.need(bank_full["act"][2 + h])
                    st.done(A(SQ[:, h, :], bank[2 + h][:, 0:T], ACT.Square), sq_ready)
                for h in range(4):
                    deviation(SQ[:, 4 + h, :], (0, 1, 6, 7)[h], "eps_rms", T, a2d)

            def bias_rows():
                for h in range(NH2):
                    copy(BBUF[:, h, :], h % 2, bank[h % 2][:, 0:384])
                mark(tbl_row)

            def convolution():
                for k in range(KD):
                    b = 3 * (k % 2) + 1
                    st.need(bank_full["act"][b])
                    if k >= 2:
                        st.need(d2a)
                    st.done(A(CV_C[:, k % 2, :], bank[b][:, 0:SEQ], ACT.Copy), bank_free["act"][b])
                    mark(a2d)
                st.need(d2a, 2)

            def attention():
                st.need(d2a)
                st.done(A(SQ[:, 0, 0:SEQ], CK, ACT.Square), a2p)
                for m in range(4):
                    copy(QI[:, m, :], 3 + m, bank[3 + m][:, 0:SEQ])
                st.need(d2a)
                st.done(A(SQ[:, 1, 0:SEQ], KX, ACT.Square), a2p)
                deviation(SQ[:, 0, 0:SEQ], 0, "eps_rms", SEQ, a2d)
                deviation(SQ[:, 1, 0:SEQ], 1, "eps_ln", SEQ, a2d)
                copy(CKT, 2, bank[2][:, 0:SEQ].rearrange("p (a b) -> p a b", a=2))
                for m in range(8):
                    copy(Q2[:, m, :], 3 + m % 4, bank[3 + m % 4][:, 0:SEQ])
                for n in range(16):
                    ns = P * (n // 8 + 1)
                    st.need(bank_full["act"][n % 2])
                    st.done(A(RL[:, n % 2, 0:ns], bank[n % 2][:, 0:ns], ACT.Relu, scale=0.125), a2d)
                for m in range(8, 16):
                    copy(Q2[:, m, :], 3 + m % 4, bank[3 + m % 4][:, 0:SEQ])
                units = [(h, t) for h in range(NH2) for t in range(2)]
                for n in range(len(units) + 3):
                    if n < len(units):
                        h, t = units[n]
                        ns = P * (t + 1)
                        st.need(d2a)
                        st.done(A(PR2[:, n % 2, 0:ns], LG2[:, n % 2, 0:ns], ACT.Exp,
                                  bias=ST2[:, n % 8, 1:2], accum_out=ST2[:, n % 8, 2:3]), a2d)
                    if 2 <= n < len(units) + 2:
                        m, t = n - 2, units[n - 2][1]
                        copy(PT2[:, m % 2, 0:t + 1, :], 2 + m % 2,
                             bank[2 + m % 2][:, 0:P * (t + 1)].rearrange("p (a b) -> p a b", b=P), a2p)
                    if n >= 3 and units[n - 3][1] == 1:
                        h = units[n - 3][0]
                        copy(O2[:, h, :], 4 + h % 2, bank[4 + h % 2][:, 0:SEQ])

            def experts(l):
                for q in range(4):
                    copy(XTOK[:, q // 2, (q % 2) * 512:(q % 2) * 512 + 512], 4 + q, bank[4 + q][:, :])
                for x in (E8, G8[:, 0:2, 0:1]):
                    st.need(d2a)
                    st.done(A(x, x, ACT.Exp), a2d)
                for q, b in ((0, 3), (1, 0)):
                    copy(ROWS[:, 2 * q:2 * q + 2, :], b, bank[b][:, :].rearrange("p (a b) -> p a b", a=2))
                mark(a2d)
                UP, TURN, DOWN = bank[4], bank[5], bank[6]
                m = M[l]

                def rows_out(b):
                    act.wait_ge(m.y, b + 1)
                    atleast(act, m.added, b)
                    A(YS[:, :], DOWN[:, :], ACT.Copy).then_inc(m.ys, 1)

                def group(i):
                    peeled = isinstance(i, int)
                    for u in range(GROUP):
                        b = GROUP * i + u
                        act.wait_ge(m.up, b + 1)
                        atleast(act, m.t, b)
                        A(HS[:, :], UP[:, :], ACT.Copy).then_inc(m.hs, 1)
                        if not (peeled and u == 0):
                            rows_out(b - 1)
                        act.wait_ge(m.t, b + 1)
                        atleast(act, m.ht, b)
                        A(SGM[:, :], TURN[:, 0:64], ACT.Silu).then_inc(m.sg, 1)

                group(0)
                rows_out(GROUP * own_and_more(act, l, group) - 1)
                for b in range(4):
                    copy(YT[:, b // 2, b % 2 * 512:b % 2 * 512 + 512], b, bank[b][:, :])

            act.wait_ge(loaded, 48)
            bias_rows()
            for l in range(2):
                ffn(first=(l == 0))
                mixer(l)
                ffn()
            rms_norm()
            convolution()
            layer_norm(0)
            experts(0)
            layer_norm(0)
            attention()
            layer_norm(4)
            experts(1)
            layer_norm(0)

        @block.vector
        def _(dve):
            st = Steps(dve, dve_step)
            v = nc.vector
            TT, TS, STT = v.tensor_tensor, v.tensor_scalar, v.scalar_tensor_tensor

            def mark(s):
                st.settle()
                st.done(dve.nop(), s)

            def then(ins, s=None):
                st.done(ins, s)
                st.settle()

            def bcast(x, n):
                return x.unsqueeze(1).to_broadcast([x.shape[0], n, x.shape[1]])

            def inner(x, n):
                return x.unsqueeze(2).to_broadcast([x.shape[0], x.shape[1], n])

            def normed(gain, at, out, s, n=T):
                st.need(std_ready)
                then(v.reciprocal(RS[:, 0:n], RS[:, 0:n]))
                for k in range(KD):
                    st.done(STT(out[:, k, 0:n], H[:, k, 0:n], small(gain)[:, at + k:at + k + 1], RS[:, 0:n],
                                ALU.mult, ALU.mult), s)

            def layer_norm(b, gain, bias, i):
                st.need(bank_full["dve"][b])
                st.done(TT(R2, R2, bcast(bank[b][:, 0:SEQ], KD), ALU.subtract), d2a)
                mark(bank_free["dve"][b])
                st.need(std_ready)
                then(v.reciprocal(RS[:, 0:SEQ], RS[:, 0:SEQ]))
                then(TT(R2, R2, bcast(RS[:, 0:SEQ], KD), ALU.mult))
                for k in range(KD):
                    at = i * KD + k
                    st.done(TS(X2[:, k, :], R2[:, k, :], small(gain)[:, at:at + 1], small(bias)[:, at:at + 1],
                               ALU.mult, ALU.add), x_tile)

            def sum_from(b, k):
                st.need(bank_full["dve"][b])
                st.done(STT(R2[:, k, :], X2[:, k, :], ALPHA, bank[b][:, 0:SEQ], ALU.mult, ALU.add), sum_tile)
                mark(bank_free["dve"][b])

            def ffn(l, j):
                normed("gains", (l * 3 + 2 * j) * KD, XN, xn_ready)
                for f in range(NF):
                    b = 2 * (f % 2) + 1
                    st.need(silu_ready)
                    st.need(bank_full["dve"][b])
                    st.done(TT(HID[:, f, :], SG[:, f % 2, :], bank[b][:, 0:T], ALU.mult), hid_ready)
                for c in range(4):
                    for dt in range(2):
                        b, k = (4 if c % 2 == 0 else 0) + dt, 2 * c + dt
                        st.need(bank_full["dve"][b])
                        st.done(STT(H[:, k, :], bank[b][:, 0:T], 0.5, H[:, k, :], ALU.mult, ALU.add), h_tile)
                        mark(bank_free["dve"][b])

            def mixer(l):
                normed("gains", (l * 3 + 1) * KD, XN, xn_ready)
                if l == 0:
                    dve.wait_ge(tbl_w, 16)
                st.need(bank_full["dve"][0])
                st.done(v.tensor_copy(LR[0:16, :], bank[0][0:16, 0:T]))
                st.done(v.tensor_copy(LR[32:48, :], bank[0][32:48, 0:T]), bank_free["dve"][0])
                for i, b in ((4, 1), (5, 2), (0, 4), (1, 5), (2, 6), (3, 7)):
                    st.need(a2d)
                    st.done(v.tensor_copy(QB[:, i, :], bank[b][:, 0:T]), bank_free["dve"][b])
                for i in range(4):
                    st.need(bank_full["dve"][4 + i])
                    st.done(TS(GT[:, i, :], bank[4 + i][:, 0:T], small("gla_b")[:, l * 4 + i:l * 4 + i + 1], None,
                               ALU.add), bank_free["dve"][4 + i])
                st.settle()
                st.done(TS(BC, GT, 0.0, None, ALU.min), d2a)
                for i in range(6):
                    st.need(a2d)
                    then(v.reciprocal(S2[:, i, :], S2[:, i, :]))
                    g = small("qn" if i < 4 else "kn")[:, l:l + 1]
                    st.done(STT(XR[:, i, :], QB[:, i, :], g, S2[:, i, :], ALU.mult, ALU.mult), d2p)
                st.settle()
                for i in range(6):
                    cos, sin = (const("cosq"), const("sinq")) if i < 4 else (const("cos"), const("sin"))
                    st.done(TT(QR[:, i, :], XR[:, i, :], cos, ALU.mult))
                    st.need(bank_full["dve"][i])
                    then(TT(QB[:, i, :], bank[i][:, 0:T], sin, ALU.mult), bank_free["dve"][i])
                    st.done(TT(QR[:, i, :], QR[:, i, :], QB[:, i, :], ALU.add), None if i < 5 else d2p)
                st.need(a2d)
                then(TT(GT, BC, EL, ALU.subtract))
                then(TS(GT, GT, 1.0 / 16.0, None, ALU.mult))
                for i in range(4):
                    st.done(v.tensor_tensor_scan(BC[:, i, :], const("restart"), GT[:, i, :], 0.0, ALU.mult, ALU.add))
                st.settle()

                def chunks(x):
                    return x[:, 0:SEQ].rearrange("p (c n) -> p c n", c=4)

                for i in range(4):
                    total = BC[:, i, 63:256:64].unsqueeze(2).to_broadcast([P, 4, 64])
                    st.done(TT(chunks(EL[:, i, :]), total, chunks(BC[:, i, :]), ALU.subtract))
                    st.done(TT(EL[:, i, SEQ:T], BC[:, i, T - 1:T].to_broadcast([P, META]), BC[:, i, SEQ:T],
                               ALU.subtract))
                then(TT(KE[:, 1], BC[:, 2:4, :], GT[:, 2:4, :], ALU.subtract))
                st.done(TT(GT[:, 2:4, :], EL[:, 2:4, :], GT[:, 2:4, :], ALU.add), d2a)
                st.need(a2d)
                for d in range(2):
                    st.done(STT(QD[:, d], QD[:, d], 0.125, QK[:, 0:2, :], ALU.mult, ALU.mult))
                    st.done(TT(KI[:, d], KI[:, d], QK[:, 2:4, :], ALU.mult))
                    st.done(TT(KE[:, d], KE[:, d], QK[:, 2:4, :], ALU.mult), gla_ready if d else None)
                units = [(h, t) for h in range(8) for t in range(3)]
                for n in range(len(units) + 2):
                    if n < len(units):
                        nt, s = TILES[units[n][1]][1], n % 8
                        st.need(bank_full["dve"][n % 2])
                        st.done(v.tensor_reduce(ST1[0:nt, s, 0:1], bank[n % 2][0:nt, 0:T], AX.X, ALU.max,
                                                negate=True), d2a)
                    if 1 <= n <= len(units):
                        m = n - 1
                        nt, s = TILES[units[m][1]][1], m % 8
                        st.need(a2d)
                        then(v.reciprocal(ST1[0:nt, s, 2:3], ST1[0:nt, s, 1:2]), bank_free["dve"][m % 2])
                        st.done(TS(PR[0:nt, m % 2, :], PR[0:nt, m % 2, :], ST1[0:nt, s, 2:3], None, ALU.mult), d2p)
                    if n >= 2:
                        m = n - 2
                        nt, b = TILES[units[m][1]][1], 2 + m % 2
                        st.need(bank_full["dve"][b])
                        src = bank[b][:, 0:256].rearrange("p (a b) -> p a b", a=2)
                        st.done(v.tensor_copy(PT[:, m % 2, 0:2, 0:nt], src[:, :, 0:nt]))
                        st.done(v.tensor_copy(PT[0:META, m % 2, 2, 0:nt], bank[b][0:META, 256:256 + nt]), d2p)
                for t, (c, nt) in enumerate(TILES):
                    st.need(bank_full["dve"][t])
                    st.done(v.tensor_copy(KET[0:nt, t], bank[t][0:nt, :].rearrange("p (a b) -> p a b", a=2)),
                            bank_free["dve"][t])
                for d, m in enumerate(("low", "high")):
                    st.need(bank_full["dve"][3 + d])
                    st.done(TT(ATT[:, d], bank[3 + d][:, :].rearrange("p (a b) -> p a b", a=8), bcast(const(m), 8),
                               ALU.mult), bank_free["dve"][3 + d])
                st.need(bank_full["dve"][5])
                for d, m in enumerate(("low", "high")):
                    st.done(TT(ATM[0:META, d].rearrange("p (a b) -> p a b", a=4),
                               bank[5][0:META, d * 64:d * 64 + 64].rearrange("p (a b) -> p a b", a=4),
                               bcast(const(m, META)[:, 0:META], 4), ALU.mult), bank_free["dve"][5] if d else None)
                for s in range(4):
                    for d in range(2):
                        b, q = (6 + s // 2, s % 2) if d == 0 else (s // 2, s % 2)
                        if q == 0:
                            st.need(bank_full["dve"][b])
                        src = bank[b][:, q * 256:q * 256 + 256]
                        free = bank_free["dve"][b] if q == 1 else None
                        if s == 0:
                            st.done(v.tensor_copy(ST[:, d, 0, :], src))
                        else:
                            c = s - 1 if d == 0 else 3 - s
                            for tile in range(2):
                                cs = slice(tile * P, tile * P + P)
                                st.done(STT(ST[:, d, s, cs], ST[:, d, s - 1, cs], DEC[:, 2 * d + tile, c:c + 1],
                                            src[:, cs], ALU.mult, ALU.add), free if tile else None)
                    st.settle()
                for h in range(4):
                    st.need(a2d)
                    then(v.reciprocal(SQ[:, 4 + h, :], SQ[:, 4 + h, :]))
                    g = small("gla_gn")[:, l * 4 + h:l * 4 + h + 1]
                    then(STT(AT[:, h, :], bank[2 + h][:, 0:T], g, SQ[:, 4 + h, :], ALU.mult, ALU.mult),
                         bank_free["dve"][2 + h])
                    st.done(TT(AT[:, h, :], AT[:, h, :], RA[:, h, :], ALU.mult), None if h < 3 else d2p)
                for k in range(KD):
                    b = 2 * (k % 2)
                    st.need(bank_full["dve"][b])
                    st.done(TT(GA[:, k, :], GA[:, k, :], bank[b][:, 0:T], ALU.mult), bank_free["dve"][b])
                    st.need(bank_full["dve"][b + 1])
                    then(TT(GB[:, k, :], GB[:, k, :], bank[b + 1][:, 0:T], ALU.mult), bank_free["dve"][b + 1])
                    st.done(TT(GA[:, k, :], GA[:, k, :], GB[:, k, :], ALU.add), None if k < KD - 1 else d2p)
                for k in range(KD):
                    b = 4 + k % 4
                    st.need(bank_full["dve"][b])
                    st.done(TT(H[:, k, :], bank[b][:, 0:T], H[:, k, :], ALU.add), h_tile)
                    mark(bank_free["dve"][b])

            def bias_rows():
                for h in range(NH2):
                    st.done(TS(BROW[0:32, h, :], const("onehot", 32), small("rel", 32)[:, h:h + 1], None, ALU.mult),
                            d2p)

            def convolution():
                st.done(v.memset(CV_U[:, :, 0:2], 0.0))
                for k in range(KD):
                    u, o, t0 = CV_U[:, k % 2, :], CV_V[:, k, :], CV_T[:, k % 2, :]
                    b = 3 * (k % 2)
                    w_ = [small("convk")[:, j * KD + k:j * KD + k + 1] for j in range(3)]
                    st.need(a2d)
                    st.need(bank_full["dve"][b + 2])
                    then(TT(u[:, 2:SEQ + 2], CV_C[:, k % 2, :], bank[b + 2][:, 0:SEQ], ALU.mult),
                         bank_free["dve"][b + 2])
                    mark(d2a)
                    then(TS(t0, u[:, 0:SEQ], w_[0], None, ALU.mult))
                    then(STT(t0, u[:, 1:SEQ + 1], w_[1], t0, ALU.mult, ALU.add))
                    then(STT(t0, u[:, 2:SEQ + 2], w_[2], t0, ALU.mult, ALU.add))
                    st.need(bank_full["dve"][b])
                    st.done(TT(o, t0, bank[b][:, 0:SEQ], ALU.mult), d2p)
                    mark(bank_free["dve"][b])
                for k in range(KD):
                    sum_from(6 + k % 2, k)

            def attention():
                st.need(bank_full["dve"][0])
                st.done(v.tensor_copy(CK, bank[0][:, 0:SEQ]), d2a)
                mark(bank_free["dve"][0])
                st.need(bank_full["dve"][1])
                st.done(v.tensor_copy(KX, bank[1][:, 0:SEQ]), d2p)
                mark(bank_free["dve"][1])
                st.need(bank_full["dve"][2])
                st.done(TS(WI, bank[2][:, 0:16].rearrange("p (a b) -> p a b", a=2), 8.0 ** -0.5, None, ALU.mult),
                        bank_free["dve"][2])
                st.need(bank_full["dve"][7])
                st.done(TT(KX, KX, bank[7][:, 0:SEQ], ALU.subtract), d2a)
                mark(bank_free["dve"][7])
                st.need(a2d)
                then(v.reciprocal(SQ[:, 0, 0:SEQ], SQ[:, 0, 0:SEQ]))
                st.done(STT(CKN, CK, small("kvg"), SQ[:, 0, 0:SEQ], ALU.mult, ALU.mult), d2p)
                st.need(a2d)
                then(v.reciprocal(SQ[:, 1, 0:SEQ], SQ[:, 1, 0:SEQ]))
                then(TT(KN2, KX, SQ[:, 1, 0:SEQ], ALU.mult))
                st.done(TS(KN2, KN2, small("kig"), small("kib"), ALU.mult, ALU.add), d2p)
                for n in range(16):
                    t, h = n // 8, n % 8
                    ns = P * (t + 1)
                    sc = SC[:, t, 0:ns]
                    acc = const("future").rearrange("p (a b) -> p a b", a=2)[:, t, 0:ns] if h == 0 else sc
                    st.need(a2d)
                    then(STT(sc, RL[:, n % 2, 0:ns], WI[:, t, h:h + 1], acc, ALU.mult, ALU.add),
                         bank_free["dve"][n % 2])
                for t in range(2):
                    ns = P * (t + 1)
                    sc, wk = SC[:, t, 0:ns], WK[:, t, 0:ns]
                    for r in range(TOPK // 8):
                        src = sc if r == 0 else wk
                        then(v.max(M8, src))
                        then(v.match_replace(wk, M8, src, LOWEST))
                    m = MSK[:, t, 0:ns]
                    then(TT(m, wk, sc, ALU.not_equal))
                    then(TT(m, m, const("causal").rearrange("p (a b) -> p a b", a=2)[:, t, 0:ns], ALU.mult))
                    then(TS(m, m, BIG, -BIG, ALU.mult, ALU.add))
                dve.wait_ge(tbl_r, 16 * 8)
                units = [(h, t) for h in range(NH2) for t in range(2)]
                for n in range(len(units) + 1):
                    if n < len(units):
                        h, t = units[n]
                        ns, s = P * (t + 1), n % 8
                        lg = LG2[:, n % 2, 0:ns]
                        st.need(bank_full["dve"][n % 2])
                        then(STT(lg, bank[n % 2][:, 0:ns], P ** -0.5, (BIAS0, BIAS1)[t][:, h, :], ALU.mult, ALU.add),
                             bank_free["dve"][n % 2])
                        then(v.tensor_tensor_reduce(out=lg, in0=lg, in1=MSK[:, t, 0:ns], scale=1.0, scalar=LOWEST,
                                                    op0=ALU.add, op1=ALU.max, accum_out=ST2[:, s, 0:1]))
                        st.done(TS(ST2[:, s, 1:2], ST2[:, s, 0:1], -1.0, None, ALU.mult), d2a)
                    if n >= 1:
                        m = n - 1
                        ns, s = P * (units[m][1] + 1), m % 8
                        st.need(a2d)
                        then(v.reciprocal(ST2[:, s, 3:4], ST2[:, s, 2:3]))
                        st.done(TS(PR2[:, m % 2, 0:ns], PR2[:, m % 2, 0:ns], ST2[:, s, 3:4], None, ALU.mult), d2p)
                for k in range(KD):
                    sum_from(6 + k % 2, k)

            def first_best(x, best, out, scr):
                then(v.tensor_reduce(best, x, AX.X, ALU.max))
                then(TT(scr, x, best.to_broadcast([P, 2, 8]), ALU.is_ge))
                then(TT(scr, scr, bcast(const("rev8"), 2), ALU.mult))
                then(v.tensor_reduce(G8[:, 0:2, 1:2], scr, AX.X, ALU.max))
                then(TT(out, scr, G8[:, 0:2, 1:2].to_broadcast([P, 2, 8]), ALU.is_equal))

            def experts(l):
                rb = small("rb")[:, l * 72:l * 72 + 72]
                gmax, v1, v2 = SLT[:, 0:2, 0:1], SLT[:, 2:4, 0:1], SLT[:, 4:6, 0:1]
                gsum = SLT[:, 6:8, 0:1]
                pay1, pay2 = SLT[:, 0:2, 1:2], SLT[:, 2:4, 1:2]
                slots = SLT[:, 4:8, 1:2]
                exv = G8[:, 0:2, 0:1]
                scr = G8[:, 2:4, :]
                st.need(bank_full["dve"][0])
                then(TT(LG, bank[0][:, 0:144].rearrange("p (a b) -> p a b", a=2), bcast(rb, 2), ALU.add),
                     bank_free["dve"][0])
                first_best(LG[:, :, 0:8], gmax, OHG, SCR8)
                st.done(TT(E8, LG[:, :, 0:8], gmax.to_broadcast([P, 2, 8]), ALU.subtract), d2a)
                for t in range(2):
                    e = LG[:, t, 8:72].rearrange("p (g e) -> p g e", g=8)
                    tm = TMP[:, t, :].rearrange("p (g e) -> p g e", g=8)
                    then(TT(tm, e, inner(OHG[:, t, :], 8), ALU.mult))
                    then(v.tensor_reduce(ES[:, t, :].unsqueeze(2), TMP[:, t, :].rearrange("p (g e) -> p e g", g=8),
                                         AX.X, ALU.add))
                first_best(ES, v1, OH[:, 0], SCR8)
                then(STT(ES, OH[:, 0], -BIG, ES, ALU.mult, ALU.add))
                first_best(ES, v2, OH[:, 1], SCR8)
                st.need(a2d)
                then(v.tensor_reduce(gsum, E8, AX.X, ALU.add))
                then(v.reciprocal(gsum, gsum))
                st.done(TT(exv, v2, v1, ALU.subtract), d2a)
                st.need(a2d)
                then(TS(pay1, exv, 1.0, None, ALU.add))
                then(v.reciprocal(pay1, pay1))
                then(TT(pay1, pay1, gsum, ALU.mult))
                then(TT(pay2, exv, pay1, ALU.mult))
                for a_ in range(2):
                    for t in range(2):
                        then(TT(MA[:, a_, t, :].rearrange("p (g e) -> p g e", g=8), inner(OHG[:, t, :], 8),
                                bcast(OH[:, a_, t, :], 8), ALU.mult))
                st.done(TT(MA[:, 2], MA[:, 0], MA[:, 1], ALU.add), d2p)
                st.need(bank_full["dve"][1])
                then(TT(CMP, inner(bank[1][:, 128:192], 8), bcast(const("steps8"), 64), ALU.is_gt))
                then(v.tensor_reduce(CNT[:, 0, :].unsqueeze(2), CMP, AX.X, ALU.add))
                then(v.tensor_tensor_scan(CNT[:, 1, :], const("one"), CNT[:, 0, :], 0.0, ALU.mult, ALU.add))
                then(TT(CNT[:, 3, :], CNT[:, 1, :], const("ident")[:, 0:64], ALU.mult))
                then(v.tensor_reduce(CNT[:, 4, 0:1], CNT[:, 3, :], AX.X, ALU.add))
                st.done(TS(CMB[0:64, :], const("blocks", 64), CNT[0:64, 4, 0:1], None, ALU.is_ge), d2p)
                then(TT(CNT[:, 2, :], CNT[:, 1, :], CNT[:, 0, :], ALU.subtract))
                then(STT(CNT[:, 2, :], CNT[:, 2, :], float(SLOTS), const("late"), ALU.mult, ALU.add))
                for t in range(2):
                    rank = bank[1][:, t * 64:t * 64 + 64]
                    then(STT(RK[:, t, :], rank, float(SLOTS), CNT[:, 2, :], ALU.is_ge, ALU.mult))
                    then(TT(RK[:, t, :], RK[:, t, :], rank, ALU.add))
                    then(TT(RK[:, t, :], RK[:, t, :], const("first"), ALU.add))
                then(TS(CNT[:, 4, 4:8], const("groups"), CNT[:, 1, NE - 1:NE], None, ALU.is_lt))
                then(v.tensor_reduce(CNT[:, 4, 8:9], CNT[:, 4, 4:8], AX.X, ALU.add))
                mark(bank_free["dve"][1])
                for a_ in range(2):
                    then(TT(TMP, MA[:, a_], RK, ALU.mult))
                    then(v.tensor_reduce(slots[:, 2 * a_:2 * a_ + 2], TMP, AX.X, ALU.add))
                for i in range(8):
                    x = (slots[:, 0:2], slots[:, 2:4], pay1, pay2)[i // 2][:, i % 2, :]
                    st.done(TS(DG[:, i, :], const("ident"), x, None, ALU.mult), d2p if i == 7 else None)
                st.need(bank_full["dve"][2])
                st.done(TS(IDS[0:1, 0:MORE], bank[2][0:1, 0:MORE], float(NE - 1), None, ALU.min))
                st.done(v.tensor_copy(IDS[0:1, MORE:MORE + 1], CNT[0:1, 4, 8:9]), ids_ready)
                st.settle()
                mark(bank_free["dve"][2])
                then(v.tensor_copy(SLC.unsqueeze(2), slots))
                for u in range(GROUP):
                    then(TS(PC[:, u:u + 1], const("row32"), float(SLOTS * u), None, ALU.add))
                st.need(a2d)
                TURN, GATHER = bank[5], bank[7]
                m = M[l]

                def select(i, done_before):
                    atleast(dve, m.ss, done_before)
                    atleast(dve, m.g_full, 2 * i)
                    for t in range(2):
                        TS(GS[:, t, :], const("iota"), SLC[:, t:t + 1], None, ALU.is_equal).then_inc(m.ss, 1)
                    dve.wait_ge(m.ss, done_before + 2)
                    for t in range(2):
                        ins = STT(GS[:, t, :], const("iota"), SLC[:, 2 + t:3 + t], GS[:, t, :], ALU.is_equal, ALU.add)
                    ins.then_inc(m.sel, 1)
                    dve.wait_ge(m.sel, i + 1)
                    TS(SLC, SLC, float(-GROUP * SLOTS), None, ALU.add).then_inc(m.ss, 1)

                select(0, 0)

                def group(i):
                    for half in range(2):
                        dve.wait_ge(m.g_full, 2 * i + half + 1)
                        if half == 0:
                            atleast(dve, m.up, GROUP * i)
                        v.tensor_copy(XG[:, 4 * half:4 * half + 4, :],
                                      GATHER[:, :].rearrange("p (a b) -> p a b", a=4)).then_inc(m.xg, 1)
                    select(i + 1, 3 + 4 * i)
                    for u in range(GROUP):
                        b = GROUP * i + u
                        atleast(dve, m.added, b - 1)
                        o = PUT[:, u % 2, :]
                        STT(o, ROWS[:, 0, :], PC[:, u:u + 1], ROWS[:, 2, :], ALU.is_equal, ALU.mult).then_inc(m.ps, 1)
                        atleast(dve, m.put, b)
                        STT(PUT2, ROWS[:, 1, :], PC[:, u:u + 1], ROWS[:, 3, :], ALU.is_equal, ALU.mult).then_inc(m.ps, 1)
                        dve.wait_ge(m.ps, 2 * b + 2)
                        TT(o, o, PUT2, ALU.add).then_inc(m.put, 1)
                        dve.wait_ge(m.sg, b + 1)
                        atleast(dve, m.y, b)
                        TT(HT, SGM, TURN[:, 64:128], ALU.mult).then_inc(m.ht, 1)
                    dve.wait_ge(m.put, GROUP * i + GROUP)
                    TS(PC, PC, float(GROUP * SLOTS), None, ALU.add).then_inc(m.ss, 1)

                group(0)
                own_and_more(dve, l, group)
                for k in range(KD):
                    sum_from(4 + k % 4, k)

            dve.wait_ge(loaded, 48)
            bias_rows()
            for l in range(2):
                ffn(l, 0)
                mixer(l)
                ffn(l, 1)
            normed("final", 0, H, x_tile, SEQ)
            convolution()
            layer_norm(0, "ln1g", "ln1b", 0)
            experts(0)
            layer_norm(0, "ln2g", "ln2b", 0)
            x_at["attention"] = st.sent[x_tile]
            attention()
            layer_norm(4, "ln1g", "ln1b", 1)
            experts(1)
            layer_norm(0, "ln2g", "ln2b", 1)
            x_at["end"] = st.sent[x_tile]

        @block.gpsimd
        def _(pool):
            skew = P * 513
            pool.wait_ge(tbl_row, 1)
            pool.dma_start(table_dram[:, 0:skew].rearrange("h (p x) -> p h x", x=513)[:, :, 0:384], BBUF
                           ).then_inc(tbl_w, 16)
            pool.wait_ge(tbl_w, 16)
            pool.wait_ge(x_tile, x_at["attention"])
            for h in range(0, NH2, 4):
                for t, dst in ((0, BIAS0), (1, BIAS1)):
                    n = P * (t + 1)
                    src = table_dram[h:h + 4, 0:P * 512].rearrange("h (p x) -> p h x", x=512)
                    pool.dma_start(dst[:, h:h + 4, :], src[:, :, 255 - P * t:255 - P * t + n]).then_inc(tbl_r, 16)

        @block.sync
        def _(sp):
            sp.dma_start(CST[:, :], cst_dram).then_inc(loaded, 16)
            sp.dma_start(SM[:, :], small_dram).then_inc(loaded, 16)
            sp.dma_start(H[:, :, :], h0_dram).then_inc(loaded, 16)

            def load_w13(l, u, e):
                v = RING_B[u][:, :].rearrange("p (k m n) -> p k m n", k=KD, m=2)
                for j, name in enumerate(("exp_w1_2", "exp_w3_2")):
                    sp.dma_start(v[:, :, j, :], w[name][l][bass.ds(e, 1)].rearrange("o (k p) n -> p (o k) n", p=P)
                                 ).then_inc(M[l].w13[u], 16)

            def load_w2(l, u, e):
                sp.dma_start(W2B[:, u, :].rearrange("p (k n) -> p k n", k=2),
                             w["exp_w2_2"][l][bass.ds(e, 1)].rearrange("o (k p) n -> p (o k) n", p=P)
                             ).then_inc(M[l].w2[u], 16)

            def expert_weights(l, i, own):
                for u in range(GROUP):
                    b = GROUP * i + u
                    e = b if own else sp.value_load(IDS[0:1, bass.ds(b - NE, 1)], min_val=0, max_val=NE - 1)
                    sp.wait_ge(M[l].up, b - GROUP + 1)
                    load_w13(l, u, e)
                    sp.wait_ge(M[l].y, b - GROUP + 1)
                    load_w2(l, u, e)

            done_moe = 0
            for label, view in plan:
                s, _, before = where[label]
                if view is None:
                    l = label[1]
                    sp.dma_start(RW[:, :, 0:8], w["router_wg_2"][l].rearrange("(k p) n -> p k n", p=P)
                                 ).then_inc(rw_ready, 16)
                    sp.dma_start(RW[:, :, 8:72], w["router_we_2"][l].rearrange("(k p) n -> p k n", p=P)
                                 ).then_inc(rw_ready, 16)
                    first = {where[x][0]: x for x in before}
                    for u in range(GROUP):
                        sp.wait_ge(*last_use[first[u]])
                        load_w13(l, u, u)
                    if l == 0:
                        sp.wait_ge(*last_use["down", 1, 1, 3, 1])
                    for u in range(GROUP):
                        load_w2(l, u, u)
                    with sp.Fori(1, NG0) as i:
                        expert_weights(l, i, own=True)
                    sp.wait_ge(ids_ready, l + 1)
                    n = NG0 + sp.value_load(IDS[0:1, MORE:MORE + 1], min_val=0, max_val=NG - NG0)
                    with sp.Fori(NG0, NG) as i:
                        with sp.If(i < n):
                            expert_weights(l, i, own=False)
                    sp.wait_ge(M[l].y, GROUP * n)
                    continue
                if before is not None:
                    sp.wait_ge(*last_use[before])
                for dst, src in view(RING_B[s]):
                    sp.dma_start(dst, src).then_inc(w_ready[s], 16)
            sp.wait_ge(x_tile, x_at["end"])
            sp.dma_start(out_dram, X2).then_inc(stored, 16)
            sp.wait_ge(stored, 16)


BIG_INPUTS = ["ffn_w_gate", "ffn_w_up", "ffn_w_down", "w_in", "w_pa", "w_pb", "w_out", "conv_w_in_2", "conv_w_out_2",
              "attn_w_in_2", "attn_w_out_2", "router_wg_2", "router_we_2", "exp_w1_2", "exp_w3_2", "exp_w2_2"]


def pack_smalls(x):
    s = small_layout()
    out = np.zeros((P, s.n), np.float32)

    def put(name, v):
        a, n = s.at[name]
        out[:v.shape[0], a:a + n] = v

    def tiles(v):
        return np.asarray(v).reshape(-1, P).T

    def twice(v):
        return np.concatenate([v, v], axis=-1).T

    put("gains", tiles(x["norm_gains"]))
    put("final", tiles(x["final_norm"]))
    put("gla_b", tiles(x["gla_b2"]))
    put("gla_gn", tiles(x["gla_gn"]))
    put("qn", twice(x["q_norm"]))
    put("kn", twice(x["k_norm"]))
    put("bmerge", tiles(x["b_merge"]))
    put("convk", tiles(x["conv_k_2"]))
    put("kvg", tiles(x["kv_norm_g_2"]))
    put("kig", twice(x["kidx_ln_g_2"]))
    put("kib", twice(x["kidx_ln_b_2"]))
    rb = np.concatenate([x["router_bg_2"], x["router_be_2"]], axis=1).reshape(1, 144)
    put("rb", np.broadcast_to(rb, (P, 144)))
    for name in ("ln1g", "ln1b", "ln2g", "ln2b"):
        put(name, tiles(x[f"{name[:3]}_{name[3]}_2"]))
    put("rel", x["rel_bias_2"])
    a, _ = s.at["gla_w"]
    for l in range(2):
        for d in range(2):
            out[32 * d:32 * d + 16, a + l * 256:a + l * 256 + 256] = x["gla_w2"][l, d]
    return out


def kernel(**inputs):
    import concourse.bacc as bacc
    from concourse.bass_utils import run_bass_kernel_spmd

    x = {k: np.asarray(v) for k, v in inputs.items()}
    nc = bacc.Bacc("TRN2", target_bir_lowering=False, num_devices=1)
    h0 = np.concatenate([x["x"][0], x["meta_tokens"]], axis=0).T.reshape(KD, P, T).transpose(1, 0, 2)
    arrays = {"cst": constants(), "smalls": pack_smalls(x), "h0": np.ascontiguousarray(h0)}
    arrays.update({f"in_{n}": np.ascontiguousarray(x[n]) for n in BIG_INPUTS})
    drams = {n: nc.dram_tensor(n, a.shape, F32, kind="ExternalInput").ap() for n, a in arrays.items()}
    w = {n: drams[f"in_{n}"] for n in BIG_INPUTS}
    table = nc.dram_tensor("bias_table", (NH2, P * 513), F32, kind="Internal").ap()
    out = nc.dram_tensor("out", (P, KD, SEQ), F32, kind="ExternalOutput").ap()
    build_model(nc, w, drams["cst"], drams["smalls"], drams["h0"], table, out)
    r = run_bass_kernel_spmd(nc, [arrays], core_ids=[0])
    got = np.asarray(r.results[0]["out"])
    return np.ascontiguousarray(got.transpose(2, 1, 0).reshape(1, SEQ, D))
```

```python
from contextlib import ExitStack

import numpy as np

import concourse.bass as bass
from concourse import mybir

ALU = mybir.AluOpType
ACT = mybir.ActivationFunctionType
AX = mybir.AxisListType
F32 = mybir.dt.float32
F32R = mybir.dt.float32r
I32 = mybir.dt.int32

P = 128
D = 1024
KD = D // P
SEQ, META = 256, 16
T = SEQ + META
TILES = [(0, 128), (128, 128), (256, 16)]
FF = 2816
NF = FF // P
EPS_RMS, EPS_LN = 1e-6, 1e-5
C_QA, C_KA, C_VA, C_RA, C_LF, C_LB, C_QB, C_KB, C_VB, C_GA, C_GB = (
    0, 256, 512, 1024, 1536, 1552, 1568, 2080, 2208, 2336, 3360)
C_Q2, C_CKV, C_QI, C_KI, C_WI, C_END2 = 0, 2048, 2176, 2688, 2752, 2760
NH2 = 16
TOPK = 64
ALPHA = 4.0 ** 0.25
BIG = 1.0e30
LOWEST = -3.0e38
NE = 64
SLOTS = 32
MORE = 16
NBLK = NE + MORE
GROUP = 4
NG0, NG = NE // GROUP, NBLK // GROUP
RING = 3
SLOT = 4096
HIGHS, CHUNK = 3, 1408


class Layout:

    def __init__(self):
        self.at, self.n = {}, 0

    def add(self, name, n):
        self.at[name] = (self.n, n)
        self.n += n

    def __call__(self, buf, name, rows=P):
        a, n = self.at[name]
        return buf[0:rows, a:a + n]


def const_layout():
    c = Layout()
    for name, n in (("ident", 128), ("ones", 128), ("mean_d", 128), ("mean128", 128), ("mean64", 128),
                    ("swap", 128), ("before", 128), ("sum4", 32), ("low", 64), ("high", 64),
                    ("cos", T), ("sin", T), ("cosq", T), ("sinq", T), ("restart", T),
                    ("causal", 512), ("future", 512), ("onehot", 384), ("rev8", 8), ("steps8", 8), ("iota", 128),
                    ("row32", 1), ("eps_rms", 1), ("eps_ln", 1), ("one", 64), ("blocks", MORE), ("first", NE), ("late", NE), ("groups", 4)):
        c.add(name, n)
    return c


def small_layout():
    s = Layout()
    for name, n in (("gains", 48), ("final", 8), ("gla_b", 8), ("gla_gn", 8), ("qn", 2), ("kn", 2),
                    ("bmerge", 32), ("convk", 24), ("kvg", 1), ("kig", 1), ("kib", 1), ("rb", 144),
                    ("ln1g", 16), ("ln1b", 16), ("ln2g", 16), ("ln2b", 16), ("rel", NH2), ("gla_w", 512)):
        s.add(name, n)
    return s


def constants():
    c = const_layout()
    out = np.zeros((P, c.n), np.float32)

    def put(name, v):
        a, n = c.at[name]
        v = np.asarray(v, np.float32)
        out[:v.shape[0], a:a + n] = v

    p = np.arange(P)
    put("ident", np.eye(P))
    put("ones", np.ones((P, P)))
    put("mean_d", np.full((P, P), 1.0 / D))
    put("mean128", np.full((P, P), 1.0 / 128))
    put("mean64", (p[:, None] // 64 == p[None] // 64) / 64.0)
    sw = np.zeros((P, P))
    for m in range(P):
        if m % 32 < 16:
            sw[m + 16, m] = -1.0
        else:
            sw[m - 16, m] = 1.0
    put("swap", sw)
    put("before", p[:, None] < p[None])
    put("sum4", (p[:, None] % 32) == np.arange(32)[None])
    put("low", (p[:, None] % 64) <= np.arange(64)[None])
    put("high", (p[:, None] % 64) >= np.arange(64)[None])
    inv = np.float32(10000.0) ** (-np.arange(0, 32, 2, dtype=np.float32) / np.float32(32))
    tok = np.arange(SEQ)
    ang = np.zeros((P, T), np.float32)
    for m in range(P):
        pos = tok // 64 if (m % 64) < 32 else tok % 64
        ang[m, :SEQ] = pos.astype(np.float32) * inv[m % 16]
    put("cos", np.cos(ang))
    put("sin", np.sin(ang))
    put("cosq", np.cos(ang) * np.float32(0.125))
    put("sinq", np.sin(ang) * np.float32(0.125))
    rs = np.ones((P, T))
    rs[:, [0, 64, 128, 192, 256]] = 0
    put("restart", rs)
    t = np.concatenate([p, p + 128]).reshape(2, P).T
    s = np.arange(SEQ)
    causal = (s[None, None] <= t[:, :, None]).astype(np.float32)
    put("causal", causal.reshape(P, 512))
    put("future", ((1 - causal) * np.float32(-BIG)).reshape(P, 512))
    dist = np.maximum(255 - np.arange(384), 0)
    f = np.maximum(dist, 1).astype(np.float32)
    large = 16 + (np.log(f / np.float32(16)) / np.float32(np.log(8.0)) * np.float32(16)).astype(np.int32)
    bucket = np.where(dist < 16, dist, np.minimum(large, 31))
    put("onehot", bucket[None] == np.arange(32)[:, None])
    put("rev8", np.tile(8 - np.arange(8), (P, 1)))
    put("steps8", np.tile(SLOTS * np.arange(1, 9), (P, 1)))
    put("iota", np.tile(np.arange(128), (P, 1)))
    put("row32", (p % 32)[:, None])
    put("eps_rms", np.full((P, 1), EPS_RMS))
    put("eps_ln", np.full((P, 1), EPS_LN))
    put("one", np.ones((P, 64)))
    put("blocks", np.tile(np.arange(MORE), (P, 1)))
    put("first", np.tile(SLOTS * np.arange(NE), (P, 1)))
    put("late", np.tile(SLOTS * (NE - 1 - np.arange(NE)), (P, 1)))
    put("groups", np.tile(GROUP * np.arange(MORE // GROUP), (P, 1)))
    return out


class MoeSignals:

    def __init__(self, w13, w2, sel, g_full, xg, up, hs, t, sg, ht, y, ys, put, added, ps, ss):
        self.w13, self.w2, self.sel, self.g_full, self.xg, self.up, self.hs, self.t = w13, w2, sel, g_full, xg, up, hs, t
        self.sg, self.ht, self.y, self.ys, self.put, self.added, self.ps, self.ss = sg, ht, y, ys, put, added, ps, ss


class Steps:

    def __init__(self, eng, own):
        self.eng, self.own, self.sent, self.seen, self.last = eng, own, {}, {}, None

    def done(self, ins, sem=None):
        sem = sem or self.own
        self.sent[sem] = self.sent.get(sem, 0) + 1
        ins.then_inc(sem, 1)
        self.last = (sem, self.sent[sem])

    def settle(self):
        self.eng.wait_ge(*self.last)

    def need(self, sem, k=1):
        self.seen[sem] = self.seen.get(sem, 0) + k
        self.eng.wait_ge(sem, self.seen[sem])


def weight_plan(w):
    plan = []

    def rows(src, a=None, b=None):
        v = src.rearrange("(k p) n -> p k n", p=P)
        return v if a is None else v[:, :, a:b]

    def cols(label, src, ranges):
        def view(buf):
            n = sum(b - a for a, b in ranges)
            v = buf[:, 0:KD * n].rearrange("p (k n) -> p k n", k=KD)
            at, out = 0, []
            for a, b in ranges:
                out.append((v[:, :, at:at + b - a], rows(src, a, b)))
                at += b - a
            return out
        plan.append((label, view))

    def ffn(l, j):
        for g in range(NF // 2):
            def up(buf, g=g):
                v = buf[:, :].rearrange("p (m k n) -> p m k n", m=2, k=KD)
                return [(v[:, 0], rows(w["ffn_w_gate"][l, j], g * 256, g * 256 + 256)),
                        (v[:, 1], rows(w["ffn_w_up"][l, j], g * 256, g * 256 + 256))]
            plan.append((("up", l, j, g), up))
        for c in range(4):
            for h in range(2):
                def down(buf, c=c, h=h):
                    v = buf[:, 0:11 * 256].rearrange("p (k n) -> p k n", k=11)
                    return [(v, rows(w["ffn_w_down"][l, j][h * 11 * P:(h + 1) * 11 * P], c * 256, c * 256 + 256))]
                plan.append((("down", l, j, c, h), down))

    def tall(label, src, kk):
        def view(buf):
            return [(buf[:, 0:kk * D].rearrange("p (k n) -> p k n", k=kk), rows(src))]
        plan.append((label, view))

    for l in range(2):
        ffn(l, 0)
        wi = w["w_in"][l]
        cols(("in3", l), wi, [(C_LF, C_QB), (C_KB, C_GA)])
        cols(("in4", l), wi, [(C_QB, C_KB)])
        cols(("in0", l), wi, [(C_QA, C_VA)])
        cols(("in1", l), wi, [(C_VA, C_RA)])
        cols(("in2", l), wi, [(C_RA, C_LF)])
        for c in range(4):
            cols(("gate", l, c), wi, [(C_GA + 512 * c, C_GA + 512 * c + 512)])
        tall(("pa", l), w["w_pa"][l], 4)
        tall(("pb", l), w["w_pb"][l], 4)
        for c in range(2):
            cols(("out", l, c), w["w_out"][l], [(512 * c, 512 * c + 512)])
        ffn(l, 1)
    for k in range(KD):
        cols(("conv", k), w["conv_w_in_2"][0], [(q * D + k * P, q * D + k * P + P) for q in range(3)])
    for c in range(2):
        cols(("convout", c), w["conv_w_out_2"][0], [(512 * c, 512 * c + 512)])
    plan.append((("moe", 0), None))
    wi = w["attn_w_in_2"][0]
    cols(("d_idx",), wi, [(C_CKV, C_QI), (C_KI, C_END2)])
    cols(("d_qi",), wi, [(C_QI, C_KI)])
    for c in range(4):
        cols(("d_q", c), wi, [(512 * c, 512 * c + 512)])
    for c in range(4):
        def view(buf, c=c):
            v = buf[:, :].rearrange("p (k n) -> p k n", k=NH2)
            return [(v, rows(w["attn_w_out_2"][0], 256 * c, 256 * c + 256))]
        plan.append((("d_out", c), view))
    plan.append((("moe", 1), None))
    return plan


def chunk_plan(plan):
    chunks = []

    def add(label, view, k, cols):
        chunks.append((label, k, cols, view))

    for label, _ in plan:
        kind = label[0]
        if kind == "up":
            for ft in range(2):
                for m in range(2):
                    add(label, lambda buf, m=m, ft=ft: buf[:, 0:SLOT].rearrange(
                        "p (m k n) -> p m k n", m=2, k=KD)[:, m, :, ft * P:(ft + 1) * P], KD, P)
        elif kind == "down":
            for dt in range(2):
                add(label, lambda buf, dt=dt: buf[:, 0:11 * 256].rearrange(
                    "p (k n) -> p k n", k=11)[:, :, dt * P:(dt + 1) * P], 11, P)
        elif kind == "conv":
            for q in (1, 2, 0):
                add(label, lambda buf, q=q: buf[:, 0:KD * 384].rearrange(
                    "p (k n) -> p k n", k=KD)[:, :, q * P:(q + 1) * P], KD, P)
        elif kind == "pa":
            for kk in range(4):
                for x in (label, ("pb", label[1])):
                    add(x, lambda buf, kk=kk: buf[:, 0:SLOT].rearrange(
                        "p (k n) -> p k n", k=4)[:, :, kk * 2 * P:(kk + 1) * 2 * P], 4, 2 * P)
        elif kind in ("out", "convout", "d_q"):
            for m in range(4):
                add(label, lambda buf, m=m: buf[:, 0:SLOT].rearrange(
                    "p (k n) -> p k n", k=KD)[:, :, m * P:(m + 1) * P], KD, P)
        elif kind == "d_out":
            for m in range(2):
                for h in range(2):
                    add(label, lambda buf, m=m, h=h: buf[:, 0:SLOT].rearrange(
                        "p (k n) -> p k n", k=NH2)[:, KD * h:KD * h + KD, m * P:(m + 1) * P], KD, P)
    return chunks


GATE_STEPS = [n for n in range(24) if n % 3 != 2]
ARENA_N = 24200


def build_model(nc, w, cst_dram, small_dram, h0_dram, table_dram, out_dram):
    CL, SL = const_layout(), small_layout()
    with ExitStack() as ctx:
        twins = {}

        def sb(name, shape, dt=F32, twin=False):
            if twin:
                with nc.sbuf_tensor(name + "_rounded", shape, F32R) as t:
                    twins[name] = t
            return ctx.enter_context(nc.sbuf_tensor(name, shape, dt))

        def rounded(view):
            return bass.AP(tensor=twins[view.tensor.name], offset=view.offset, ap=view.ap)

        def part(view):
            return rounded(view).bitcast(F32)

        def sem(name):
            return ctx.enter_context(nc.semaphore(name))

        CST, SM = sb("CST", [P, CL.n]), sb("SM", [P, SL.n])
        H = sb("H", [P, KD, T])
        XN = sb("XN", [P, KD, T], twin=True)
        SQ = sb("SQ", [P, KD, T], twin=True)
        RS = sb("RS", [P, T])
        RW = sb("RW", [P, KD, 72])
        IDS = sb("IDS", [1, MORE + 1], I32)
        RING_B = [sb(f"wring{i}", [P, SLOT], twin=True) for i in range(RING)]
        RING_B.append(sb("wring3", [P, HIGHS * CHUNK], twin=True))
        ARENA = sb("ARENA", [P, ARENA_N], twin=True)
        bank = [ctx.enter_context(nc.psum_tensor(f"bank{i}", [P, 512], F32)) for i in range(8)]
        X2, R2 = H[:, :, 0:SEQ], XN[:, :, 0:SEQ]

        def const(name, rows=P):
            return CL(CST, name, rows)

        def small(name, rows=P):
            return SL(SM, name, rows)

        class Arena:

            def __init__(self, start=0):
                self.n = start

            def __call__(self, *shape):
                n = int(np.prod(shape))
                v = ARENA[:, self.n:self.n + n]
                self.n += n
                assert self.n <= ARENA_N, self.n
                names = "abcd"[:len(shape)]
                kw = {names[i]: shape[i] for i in range(1, len(shape))}
                return v.rearrange(f"p ({' '.join(names)}) -> p {' '.join(names)}", **kw) if kw else v

        bank_full = {e: [sem(f"bank{b}_full_{e}") for b in range(8)] for e in ("act", "dve")}
        bank_free = {e: [sem(f"bank{b}_free_{e}") for b in range(8)] for e in ("act", "dve")}
        act_step, dve_step = sem("act_step"), sem("dve_step")
        w_ready = [sem(f"w_ready{i}") for i in range(RING)]
        half_used = sem("half_sum_done")
        wh_ready, wl_ready = sem("weights_high_ready"), sem("weights_low_ready")
        x_made, xh_ready, xl_ready = sem("split_input_ready"), sem("input_high_ready"), sem("input_low_ready")
        xa_ready, o_made = sem("attention_input_high_ready"), sem("head_output_ready")
        x_at = {}
        loaded = sem("loaded")
        rw_ready = sem("router_weights_ready")
        h_tile = sem("h_tile")
        sum_tile = sem("sum_tile")
        x_tile = sem("x_tile")
        sq_ready = sem("sq_ready")
        std_ready = sem("std_ready")
        xn_ready = sem("xn_ready")
        silu_ready = sem("silu_ready")
        hid_ready = sem("hid_ready")
        a2d, a2p = sem("act_result_for_dve"), sem("act_result_for_pe")
        d2a, d2p = sem("dve_result_for_act"), sem("dve_result_for_pe")
        rows_done = sem("products_from_other_rows_done")
        pv_done = sem("values_product_done")
        gla_ready = sem("decayed_keys_ready")
        tbl_row, tbl_w, tbl_r = sem("bias_row_ready"), sem("bias_table_written"), sem("bias_table_read")
        ids_ready = sem("ids_ready")
        M = []
        for l in range(2):
            M.append(MoeSignals(
                w13=[sem(f"moe{l}_w13_ready{i}") for i in range(GROUP)],
                w2=[sem(f"moe{l}_w2_ready{i}") for i in range(GROUP)],
                **{k: sem(f"moe{l}_{name}") for k, name in (
                    ("sel", "select_ready"), ("g_full", "gather_full"), ("xg", "gathered"), ("up", "up_full"),
                    ("hs", "up_copied"), ("t", "turned"), ("sg", "silu_ready"), ("ht", "hidden_ready"),
                    ("y", "down_full"), ("ys", "down_copied"), ("put", "put_ready"), ("added", "added"),
                    ("ps", "put_step"), ("ss", "select_step"))}))
        stored = sem("stored")

        plan = weight_plan(w)
        where, count, owner, n = {}, [0] * RING, [None] * RING, 0
        for label, view in plan:
            if view is None:
                where[label] = (0, 0, owner + [before_it])
                n, owner = 0, [None] * RING
                continue
            s = n % RING
            n += 1
            count[s] += 16 * len(view(RING_B[s]))
            where[label] = (s, count[s], owner[s])
            owner[s] = before_it = label
        chunks = chunk_plan(plan)

        def chunk_views(c):
            label, k, n, view = chunks[c]
            at = c % HIGHS * CHUNK
            high = RING_B[RING][:, at:at + k * n].rearrange("p (k n) -> p k n", k=k)
            return view(RING_B[where[label][0]]), high

        chunk_use = {}
        last_use = {}

        a = Arena()
        HID, SG = a(NF, T), a(2, T)
        HIDH = Arena(a.n)(NF, T)
        BROW, BBUF = a(NH2, 384), a(NH2, 384)
        a = Arena()
        QK, VA, RA, LR, VB = a(4, T), a(3, 512), a(4, T), a(T), a(3, 128)
        QR, GA, GB, BT, AT = a(6, T), a(KD, T), a(KD, T), a(4, T), a(4, T)
        PR, PT, ST1 = a(3, T), a(2, 3, 128), a(8, 4)
        GT, BC, EL = a(4, T), a(4, T), a(4, T)
        QB, XR = Arena(a.n)(6, T), Arena(a.n + 6 * T)(6, T)
        QD, KI, KE = a(2, 2, T), a(2, 2, T), a(2, 2, T)
        BTH, ATH, GAH = GT, BC, GB
        KET = SQ[:, 0:6, :].rearrange("p a b -> p (a b)")[:, 0:1536].rearrange("p (a b c) -> p a b c", a=3, b=2)
        ST = a(2, 4, 256)
        ATT, ATM, DEC = a(2, 8, 64), a(2, 64), a(4, 4)
        S2 = SQ[:, 0:6, :]
        a = Arena()
        CV_C, CV_U, CV_T, CV_V, CV_H = a(2, SEQ), a(2, SEQ + 2), a(2, SEQ), a(KD, SEQ), a(KD, SEQ)
        a = Arena()
        CK, CKN, CKT, KX, KN2, WI = a(SEQ), a(SEQ), a(2, P), a(SEQ), a(SEQ), a(2, 8)
        QI, Q2, O2 = a(4, SEQ), a(NH2, SEQ), a(NH2, SEQ)
        MSK = a(2, SEQ)
        SC, WK = Arena(a.n)(2, SEQ), Arena(a.n + 2 * SEQ)(2, SEQ)
        O2H = a(NH2, SEQ)
        BIAS0, BIAS1 = a(NH2, P), a(NH2, SEQ)
        RL, LG2, PR2, PT2, M8, ST2 = a(2, SEQ), a(2, SEQ), a(3, SEQ), a(2, 2, P), a(8), a(8, 4)
        a = Arena()
        XTOK, XG, HS, YS, SGM, HT, PUT, PUT2 = a(2, D), a(KD, P), a(512), a(512), a(64), a(64), a(2, SEQ), a(SEQ)
        LG, E8, G8, OHG, ES, OH = a(2, 72), a(2, 8), a(8, 2), a(2, 8), a(2, 8), a(2, 2, 8)
        TMP, MA, RK, CMP, CNT, SLT = a(2, 64), a(3, 2, 64), a(2, 64), a(64, 8), a(5, 64), a(8, 2)
        DG, ROWS, GS, PC, SLC, CMB = a(8, P), a(4, SEQ), a(2, P), a(GROUP), a(4), a(MORE)
        YT, SCR8 = a(2, D), a(2, 8)
        W2B = a(GROUP, 2048)

        block = ctx.enter_context(nc.Block())

        def atleast(eng, s, value):
            if not isinstance(value, int) or value > 0:
                eng.wait_ge(s, value)

        def own_and_more(eng, l, group):
            with eng.Fori(1, NG0) as i:
                group(i)
            eng.wait_ge(ids_ready, l + 1)
            n = NG0 + eng.value_load(IDS[0:1, MORE:MORE + 1], min_val=0, max_val=NG - NG0)
            with eng.Fori(NG0, NG) as i:
                with eng.If(i < n):
                    group(i)
            return n
        @block.tensor
        def _(pe):
            st = Steps(pe, None)
            held = {}

            def claim(b):
                if b in held:
                    st.need(bank_free[held.pop(b)][b])

            def products(b, reader, freer, groups):
                claim(b)
                for g in groups:
                    if g is None:
                        st.done(ins, rows_done)
                        st.settle()
                        continue
                    for i, (o, l, r) in enumerate(g):
                        ins = nc.tensor.matmul(o, l, r, start=(i == 0), stop=(i == len(g) - 1))
                st.done(ins, bank_full[reader][b])
                if freer:
                    held[b] = freer

            def turns(b, reader, freer, items):
                claim(b)
                for o, i in items:
                    n = i.shape[0]
                    ins = nc.tensor.transpose(o, i, const("ident", n)[:, 0:n])
                st.done(ins, bank_full[reader][b])
                if freer:
                    held[b] = freer

            def slot(label):
                s, ready, _ = where[label]
                pe.wait_ge(w_ready[s], ready)
                return RING_B[s]

            def used(label):
                last_use[label] = st.last

            progress = {"chunk": 0}

            def split_sum(o, tiles, start=True, stop=True, before=None, cols=slice(0, P), again=False):
                if not again:
                    progress["chunk"] += 1
                c = progress["chunk"] - 1
                low, high = chunk_views(c)
                pe.wait_ge(wl_ready, c + 1)
                for k, (xh, xl) in enumerate(tiles):
                    if before:
                        before(k)
                    for j, (a_, x) in enumerate(((low, xh), (high, xl), (high, xh))):
                        ins = nc.tensor.matmul(o, rounded(a_[:, k, cols]), rounded(x),
                                               start=(start and k == 0 and j == 0),
                                               stop=(stop and k == len(tiles) - 1 and j == 2))
                return ins

            def chunk_done(ins, s):
                st.done(ins, s)
                chunk_use[progress["chunk"] - 1] = st.last
                last_use[chunks[progress["chunk"] - 1][0]] = st.last

            def split_products(b, reader, tiles):
                claim(b)
                n = tiles[0][0].shape[1]
                chunk_done(split_sum(bank[b][:, 0:n], tiles), bank_full[reader][b])
                held[b] = reader

            def cols_of(label, n):
                return slot(label)[:, 0:KD * n].rearrange("p (k n) -> p k n", k=KD)

            def rows(x, n=T):
                return [x[:, k, 0:n] for k in range(KD)]

            def pairs(high, low, n, m=T):
                return [(high[:, k, 0:m], low[:, k, 0:m]) for k in range(n)]

            def column_means(b, wgt, tiles, reader):
                claim(b)
                for k, x in enumerate(tiles):
                    st.need(sq_ready)
                    ins = nc.tensor.matmul(bank[b][:, 0:x.shape[1]], const(wgt), x, start=(k == 0),
                                           stop=(k == len(tiles) - 1))
                st.done(ins, bank_full[reader][b])

            def rms_norm():
                column_means(7, "mean_d", rows(SQ), "act")

            def layer_norm(b):
                claim(b)
                for k in range(KD):
                    st.need(sum_tile)
                    ins = nc.tensor.matmul(bank[b][:, 0:SEQ], const("mean_d"), R2[:, k, :], start=(k == 0),
                                           stop=(k == KD - 1))
                st.done(ins, bank_full["dve"][b])
                held[b] = "dve"
                column_means(b + 1, "mean_d", rows(SQ, SEQ), "act")
                st.need(x_tile, KD)

            def ffn(l, j):
                rms_norm()
                tiles = pairs(SQ, XN, KD)
                for f in range(NF):
                    pair = 2 * (f % 2)
                    if f >= 2:
                        st.need(hid_ready)
                    for m, e in ((0, "act"), (1, "dve")):
                        claim(pair + m)
                        ins = split_sum(bank[pair + m][:, 0:T], tiles,
                                        before=(lambda k: st.need(xn_ready)) if f == 0 and m == 0 else None)
                        chunk_done(ins, bank_full[e][pair + m])
                tiles = pairs(HIDH, HID, NF)
                for c in range(4):
                    for h in range(2):
                        for dt in range(2):
                            b = (4 if c % 2 == 0 else 0) + dt
                            if h == 0:
                                claim(b)
                            last_hidden = lambda f: st.need(hid_ready) if f >= 9 else None
                            ins = split_sum(bank[b][:, 0:T], tiles[h * 11:h * 11 + 11], start=(h == 0), stop=(h == 1),
                                            before=last_hidden if (c, h, dt) == (0, 1, 0) else None)
                            if h == 1:
                                chunk_done(ins, bank_full["dve"][b])
                                held[b] = "dve"
                            else:
                                chunk_done(ins, half_used)

            def gate_tile(l, g):
                v = cols_of(("gate", l, g // 4), 512)
                b, m = 6 + g % 2, g % 4
                products(b, "act", "act",
                         [[(bank[b][:, 0:T], v[:, k, m * P:(m + 1) * P], x) for k, x in enumerate(rows(XN))]])
                if m == 3:
                    used(("gate", l, g // 4))

            def mixer(l):
                rms_norm()
                st.need(xn_ready, KD)
                v = cols_of(("in3", l), 288)
                products(0, "dve", "dve",
                         [[(bank[0][32 * d:32 * d + 16, 0:T], v[:, k, 16 * d:16 * d + 16], x)
                           for k, x in enumerate(rows(XN))] for d in range(2)])
                for kv in range(2):
                    products(1 + kv, "act", "dve",
                             [[(bank[1 + kv][64 * half:64 * half + 64, 0:T], v[:, k, 32 + 64 * kv:96 + 64 * kv], x)
                               for k, x in enumerate(rows(XN))] for half in range(2)])
                products(3, "act", "act",
                         [[(bank[3][0:nt, t * P:(t + 1) * P], XN[:, k, a:a + nt], v[:, k, 160:288])
                           for k in range(KD)] for t, (a, nt) in enumerate(TILES)])
                used(("in3", l))
                v = cols_of(("in4", l), 512)
                for m in range(4):
                    products(4 + m, "act", "dve",
                             [[(bank[4 + m][:, 0:T], v[:, k, m * P:(m + 1) * P], x) for k, x in enumerate(rows(XN))]])
                used(("in4", l))
                v = cols_of(("in0", l), 512)
                for m in range(4):
                    products(m, "act", "act",
                             [[(bank[m][:, 0:T], v[:, k, m * P:(m + 1) * P], x) for k, x in enumerate(rows(XN))]])
                used(("in0", l))
                for i in range(4):
                    d, tile = i // 2, i % 2
                    products(4 + i, "dve", "dve",
                             [[(bank[4 + i][:, 0:T],
                                small("gla_w")[32 * d:32 * d + 16, l * 256 + tile * P:l * 256 + tile * P + P],
                                LR[32 * d:32 * d + 16, :])]])
                for i in range(6):
                    products(i, "act", None, [[(bank[i][:, 0:T], const("mean64"), S2[:, i, :])]])
                v = cols_of(("in1", l), 512)
                for t, (a_, nt) in enumerate(TILES):
                    b = (6, 7, 6)[t]
                    products(b, "act", "act",
                             [[(bank[b][0:nt, :], XN[:, k, a_:a_ + nt], v[:, k, :]) for k in range(KD)]])
                used(("in1", l))
                for i in range(6):
                    st.need(d2p)
                    products(i, "dve", "dve", [[(bank[i][:, 0:T], const("swap"), XR[:, i, :])]])
                v = cols_of(("in2", l), 512)
                for m in range(4):
                    b = (6, 7)[m % 2]
                    products(b, "act", "act",
                             [[(bank[b][:, 0:T], v[:, k, m * P:(m + 1) * P], x) for k, x in enumerate(rows(XN))]])
                used(("in2", l))
                st.need(d2p)
                units = [(h, t) for h in range(8) for t in range(3)]

                def scores(n):
                    h, t = units[n]
                    a_, nt = TILES[t]
                    hp = 64 * (h % 2)
                    products(n % 2, "dve", "dve",
                             [[(bank[n % 2][0:nt, 0:T], QR[hp:hp + 64, h // 2, a_:a_ + nt],
                                QR[hp:hp + 64, 4 + h // 4, :])]])

                def turn_rows(n):
                    h, t = units[n]
                    nt = TILES[t][1]
                    st.need(d2p)
                    turns(2 + n % 2, "dve", None,
                          [(bank[2 + n % 2][0:nk, kt * P:kt * P + nt], PR[0:nt, n % 3, c:c + nk])
                           for kt, (c, nk) in enumerate(TILES)])

                def values(n):
                    h, t = units[n]
                    a_, nt = TILES[t]
                    st.need(d2p)
                    hp, b = 64 * (h % 2), 4 + h // 2 % 2
                    if t == 0 and h % 2 == 0:
                        claim(b)
                    for kt, (c, nk) in enumerate(TILES):
                        ins = nc.tensor.matmul(bank[b][hp:hp + 64, a_:a_ + nt],
                                               VB[0:nk, kt, 64 * (h // 4):64 * (h // 4) + 64],
                                               PT[0:nk, n % 2, kt, 0:nt], start=(kt == 0), stop=(kt == 2))
                    if t == 2 and h % 2 == 1:
                        st.done(ins, bank_full["act"][b])
                        held[b] = "act"
                    else:
                        st.done(ins, pv_done)

                scores(0)
                for n in range(len(units) + 2):
                    if n + 1 < len(units):
                        scores(n + 1)
                    if 1 <= n <= len(units):
                        turn_rows(n - 1)
                    if n >= 2:
                        values(n - 2)
                    if n in GATE_STEPS:
                        gate_tile(l, GATE_STEPS.index(n))
                st.need(gla_ready)
                for t, (c, nt) in enumerate(TILES):
                    turns(t, "dve", "dve",
                          [(bank[t][0:nt, i * P:(i + 1) * P], KE[:, i // 2, i % 2, c:c + nt]) for i in range(4)])
                for d in range(2):
                    g = []
                    for h in (0, 2, 1, 3):
                        hp = 64 * (h % 2)
                        if h == 1:
                            g.append(None)
                        for t in range(2):
                            for c in range(2):
                                at = t * P + c * 64
                                g.append([(bank[3 + d][64 * c:64 * c + 64, (2 * h + t) * 64:(2 * h + t) * 64 + 64],
                                           KI[hp:hp + 64, d, h // 2, at:at + 64], QD[hp:hp + 64, d, h // 2, at:at + 64])])
                    products(3 + d, "dve", "dve", g)
                def meta_scores(d, h):
                    return [(bank[5][0:META, d * 64 + h * META:d * 64 + h * META + META],
                             KI[64 * (h % 2):64 * (h % 2) + 64, d, h // 2, SEQ:T],
                             QD[64 * (h % 2):64 * (h % 2) + 64, d, h // 2, SEQ:T])]

                products(5, "dve", "dve", [meta_scores(d, h) for d in range(2) for h in (0, 2)] + [None]
                         + [meta_scores(d, h) for d in range(2) for h in (1, 3)])
                for b in range(3):
                    claim(b)
                for d, steps in ((0, (4, 0, 1, 2)), (1, (3, 2, 1, 0))):
                    for half in range(2):
                        b = 6 + half if d == 0 else half
                        g = []
                        for q in range(2):
                            c = steps[2 * half + q]
                            r0, nr, t = (0, META, 2) if c == 4 else (64 * (c % 2), 64, c // 2)
                            if q == 1:
                                g.append(None)
                            for h in range(4):
                                g.append([(bank[b][64 * (h % 2):64 * (h % 2) + 64,
                                                   q * 256 + h // 2 * P:q * 256 + h // 2 * P + P],
                                           KET[r0:r0 + nr, t, d, h * 64:h * 64 + 64],
                                           VA[r0:r0 + nr, t, h * P:h * P + P])])
                        products(b, "dve", "dve", g)
                for b in (3, 4, 5, 6, 7, 0, 1):
                    claim(b)
                for h in range(4):
                    hp, by_row = 64 * (h % 2), {0: [], 64: []}
                    tile = slice(h // 2 * P, h // 2 * P + P)
                    for c in range(4):
                        r0, t, at = 64 * (c % 2), c // 2, c * 64
                        o = bank[2 + h][:, at:at + 64]
                        for d in range(2):
                            by_row[r0].append((o, VA[r0:r0 + 64, t, h * P:h * P + P], ATT[r0:r0 + 64, d, 2 * h + t, :]))
                        by_row[hp].append((o, ST[hp:hp + 64, 0, c, tile], QD[hp:hp + 64, 0, h // 2, at:at + 64]))
                        if c < 3:
                            by_row[hp].append((o, ST[hp:hp + 64, 1, 2 - c, tile], QD[hp:hp + 64, 1, h // 2, at:at + 64]))
                    o = bank[2 + h][:, SEQ:T]
                    for d in range(2):
                        by_row[0].append((o, VA[0:META, 2, h * P:h * P + P], ATM[0:META, d, h * META:h * META + META]))
                    by_row[hp].append((o, ST[hp:hp + 64, 1, 3, tile], QD[hp:hp + 64, 1, h // 2, SEQ:T]))
                    claim(2 + h)
                    for r0 in (0, 64):
                        for i, (o, l_, r_) in enumerate(by_row[r0]):
                            ins = nc.tensor.matmul(o, l_, r_, start=(r0 == 0 and i == 0),
                                                   stop=(r0 == 64 and i == len(by_row[64]) - 1), skip_group_check=True)
                        if r0 == 0:
                            st.done(ins, rows_done)
                            st.settle()
                    st.done(ins, bank_full["act"][2 + h])
                    held[2 + h] = "dve"
                for h in range(4):
                    b = (0, 1, 6, 7)[h]
                    st.need(sq_ready)
                    products(b, "act", None, [[(bank[b][:, 0:T], const("mean128"), SQ[:, h, :])]])
                st.need(d2p)
                st.need(xl_ready, 4)
                for kk in range(4):
                    for m, tiles in enumerate((pairs(ATH, AT, 4), pairs(BTH, BT, 4))):
                        for i in range(2):
                            b = 2 * i + m
                            claim(b)
                            chunk_done(split_sum(bank[b][:, 0:T], tiles, cols=slice(i * P, i * P + P), again=(i == 1)),
                                       bank_full["dve"][b])
                            held[b] = "dve"
                st.need(d2p)
                for k in range(KD):
                    split_products(4 + k % 4, "dve", pairs(GAH, GA, KD))

            def bias_rows():
                for h in range(NH2):
                    st.need(d2p)
                    products(h % 2, "act", "act",
                             [[(bank[h % 2][:, 0:384], const("ones", 32), BROW[0:32, h, :])]])

            def convolution():
                st.need(x_tile, KD)
                for k in range(KD):
                    for q, e in ((1, "act"), (2, "dve"), (0, "dve")):
                        split_products(3 * (k % 2) + q, e, pairs(SQ, XN, KD, SEQ))
                st.need(d2p, KD)
                for c in range(2):
                    for m in range(4):
                        split_products(6 + m % 2, "dve", pairs(CV_H, CV_V, KD, SEQ))

            def attention():
                v = cols_of(("d_idx",), 200)
                xs = rows(X2, SEQ)
                products(0, "dve", "dve", [[(bank[0][:, 0:SEQ], v[:, k, 0:P], x) for k, x in enumerate(xs)]])
                products(1, "dve", "dve",
                         [[(bank[1][64 * half:64 * half + 64, 0:SEQ], v[:, k, P:P + 64], x)
                           for k, x in enumerate(xs)] for half in range(2)])
                products(2, "dve", "dve",
                         [[(bank[2][:, 8 * t:8 * t + 8], X2[:, k, t * P:(t + 1) * P], v[:, k, 192:200])
                           for k in range(KD)] for t in range(2)])
                used(("d_idx",))
                v = cols_of(("d_qi",), 512)
                for m in range(4):
                    products(3 + m, "act", "act",
                             [[(bank[3 + m][:, 0:SEQ], v[:, k, m * P:(m + 1) * P], x) for k, x in enumerate(xs)]])
                used(("d_qi",))
                st.need(d2p)
                products(7, "dve", "dve", [[(bank[7][:, 0:SEQ], const("mean64"), KX)]])
                st.need(a2p)
                products(0, "act", None, [[(bank[0][:, 0:SEQ], const("mean128"), LG2[:, 0, :])]])
                st.need(a2p)
                products(1, "act", None, [[(bank[1][:, 0:SEQ], const("mean64"), LG2[:, 1, :])]])
                st.need(d2p)
                turns(2, "act", "act", [(bank[2][:, t * P:(t + 1) * P], CKN[:, t * P:(t + 1) * P]) for t in range(2)])
                st.need(xl_ready)
                for q in range(8):
                    split_products(3 + q % 4, "act", pairs(SQ, XN, KD, SEQ))
                st.need(d2p)
                for n in range(16):
                    t, h = n // 8, n % 8
                    hp = 64 * (h % 2)
                    products(n % 2, "act", "dve",
                             [[(bank[n % 2][:, 0:P * (t + 1)], QI[hp:hp + 64, h // 2, t * P:(t + 1) * P],
                                KN2[hp:hp + 64, 0:P * (t + 1)])]])
                for q in range(8):
                    split_products(3 + q % 4, "act", pairs(SQ, XN, KD, SEQ))
                for b in range(2, 7):
                    claim(b)
                units = [(h, t) for h in range(NH2) for t in range(2)]

                def scores(n):
                    h, t = units[n]
                    products(n % 2, "dve", "dve",
                             [[(bank[n % 2][:, 0:P * (t + 1)], Q2[:, h, t * P:(t + 1) * P], CKN[:, 0:P * (t + 1)])]])

                def turn_rows(n):
                    h, t = units[n]
                    st.need(d2p)
                    turns(2 + n % 2, "act", None,
                          [(bank[2 + n % 2][:, s * P:(s + 1) * P], PR2[:, n % 3, s * P:(s + 1) * P])
                           for s in range(t + 1)])

                def values(n):
                    h, t = units[n]
                    st.need(a2p)
                    b = 4 + h % 2
                    if t == 0:
                        claim(b)
                    for s in range(t + 1):
                        ins = nc.tensor.matmul(bank[b][:, t * P:(t + 1) * P], CKT[:, s, :], PT2[:, n % 2, s, :],
                                               start=(s == 0), stop=(s == t))
                    if t == 1:
                        st.done(ins, bank_full["act"][b])
                        held[b] = "act"
                    else:
                        st.done(ins, pv_done)

                scores(0)
                for n in range(len(units) + 2):
                    if n + 1 < len(units):
                        scores(n + 1)
                    if 1 <= n <= len(units):
                        turn_rows(n - 1)
                    if n >= 2:
                        values(n - 2)
                for b in (4, 5):
                    claim(b)
                st.need(xl_ready, NH2)
                tiles = pairs(O2H, O2, NH2, SEQ)
                for c in range(4):
                    for m in range(2):
                        b = 6 + m
                        claim(b)
                        chunk_done(split_sum(bank[b][:, 0:SEQ], tiles[0:KD], stop=False), half_used)
                        chunk_done(split_sum(bank[b][:, 0:SEQ], tiles[KD:], start=False), bank_full["dve"][b])
                        held[b] = "dve"

            def experts(l):
                pe.wait_ge(rw_ready, 32 * (l + 1))
                products(0, "dve", "dve",
                         [[(bank[0][:, t * 72:(t + 1) * 72], X2[:, k, t * P:(t + 1) * P], RW[:, k, :])
                           for k in range(KD)] for t in range(2)])
                for q in range(4):
                    turns(4 + q, "act", "act",
                          [(bank[4 + q][:, kk * P:(kk + 1) * P],
                            X2[:, (q % 2) * 4 + kk, q // 2 * P:(q // 2 + 1) * P]) for kk in range(4)])
                st.need(d2p)
                B = bank[1]
                products(1, "dve", "dve",
                         [[(B[:, 0:64], const("before"), MA[:, 2, 0, :])],
                          [(B[:, 64:128], const("ones"), MA[:, 2, 0, :]), (B[:, 64:128], const("before"), MA[:, 2, 1, :])],
                          [(B[:, 128:192], const("ones"), MA[:, 2, 0, :]), (B[:, 128:192], const("ones"), MA[:, 2, 1, :])]])
                st.need(d2p)
                products(2, "dve", "dve", [[(bank[2][:, 0:MORE], const("ones", 64), CMB[0:64, :])]])
                st.need(d2p)
                for q in range(2):
                    products((3, 0)[q], "act", "act",
                             [[(bank[(3, 0)[q]][:, i * P:(i + 1) * P], const("ones"), DG[:, 4 * q + i, :])]
                              for i in range(4)])
                for b in list(held):
                    claim(b)
                UP, TURN, DOWN, GATHER = bank[4], bank[5], bank[6], bank[7]
                m = M[l]

                def gather(i):
                    pe.wait_ge(m.sel, i + 1)
                    for half in range(2):
                        atleast(pe, m.xg, 2 * i + half)
                        for kk in range(4):
                            k = 4 * half + kk
                            for t in range(2):
                                ins = nc.tensor.matmul(GATHER[:, kk * P:(kk + 1) * P], XTOK[:, t, k * P:(k + 1) * P],
                                                       GS[:, t, :], start=(t == 0), stop=(t == 1))
                        ins.then_inc(m.g_full, 1)
                    pe.wait_ge(m.xg, 2 * i + 2)

                def down(b, u, i):
                    pe.wait_ge(m.ht, b + 1)
                    pe.wait_ge(m.w2[u], 16 * (i + 1))
                    atleast(pe, m.ys, b)
                    w2 = W2B[:, u, :].rearrange("p (k n) -> p k n", k=2)
                    for q in range(4):
                        dh, c = q // 2, q % 2
                        ins = nc.tensor.matmul(DOWN[32 * q:32 * q + 32, :], HT[:, c * 32:c * 32 + 32],
                                               w2[:, c, dh * 512:dh * 512 + 512], start=True, stop=True,
                                               tile_position=(0, 32 * q))
                    ins.then_inc(m.y, 1)

                def put(b, u, first, last):
                    pe.wait_ge(m.ys, b + 1)
                    pe.wait_ge(m.put, b + 1)
                    for t in range(2):
                        for dh in range(2):
                            ins = nc.tensor.matmul(bank[2 * t + dh][:, :], PUT[64 * dh:64 * dh + 64, u % 2, t * P:(t + 1) * P],
                                                   YS[64 * dh:64 * dh + 64, :], start=first, stop=last,
                                                   skip_group_check=True)
                    ins.then_inc(m.added, 1)

                def group(i):
                    peeled = isinstance(i, int)
                    gather(i)
                    for u in range(GROUP):
                        b = GROUP * i + u
                        pe.wait_ge(m.w13[u], 32 * (i + 1))
                        atleast(pe, m.hs, b)
                        v = RING_B[u][:, 0:SLOT].rearrange("p (k n) -> p k n", k=KD)
                        for k in range(KD):
                            q = k % 4
                            ins = nc.tensor.matmul(UP[32 * q:32 * q + 32, :], XG[:, k, u * 32:u * 32 + 32], v[:, k, :],
                                                   start=(k < 4), stop=(k >= 4), tile_position=(0, 32 * q))
                        ins.then_inc(m.up, 1)
                        if not (peeled and u == 0):
                            down(b - 1, (u - 1) % GROUP, i if u else i - 1)
                        pe.wait_ge(m.hs, b + 1)
                        atleast(pe, m.ht, b)
                        for f in range(4):
                            ins = nc.tensor.matmul(TURN[:, f * 32:f * 32 + 32], HS[:, f * P:(f + 1) * P], const("sum4"),
                                                   start=True, stop=True)
                        ins.then_inc(m.t, 1)
                        if not (peeled and u == 0):
                            put(b - 1, (u - 1) % GROUP, peeled and u == 1, False)

                group(0)
                n = own_and_more(pe, l, group)
                down(GROUP * n - 1, GROUP - 1, n - 1)
                pe.wait_ge(m.ys, GROUP * n)
                pe.wait_ge(m.put, GROUP * n)
                for b in range(4):
                    t, dh = b // 2, b % 2
                    ins = nc.tensor.matmul(bank[b][:, :], PUT[64 * dh:64 * dh + 64, (GROUP - 1) % 2, t * P:(t + 1) * P],
                                           YS[64 * dh:64 * dh + 64, :], start=False, stop=True, skip_group_check=True)
                    st.done(ins, bank_full["act"][b])
                    held[b] = "act"
                for b in range(4):
                    claim(b)
                for k in range(KD):
                    turns(4 + k % 4, "dve", "dve",
                          [(bank[4 + k % 4][:, t * P:(t + 1) * P], YT[:, t, k * P:(k + 1) * P]) for t in range(2)])

            pe.wait_ge(loaded, 48)
            bias_rows()
            for l in range(2):
                ffn(l, 0)
                mixer(l)
                ffn(l, 1)
            rms_norm()
            convolution()
            layer_norm(0)
            experts(0)
            layer_norm(0)
            attention()
            layer_norm(4)
            experts(1)
            layer_norm(0)

        @block.scalar
        def _(act):
            st = Steps(act, act_step)
            A = nc.scalar.activation

            def mark(s):
                st.settle()
                st.done(act.nop(), s)

            def copy(out, b, view, s=None):
                st.need(bank_full["act"][b])
                st.done(A(out, view, ACT.Copy), s or bank_free["act"][b])

            progress = {"chunk": 0}

            def high_part():
                c = progress["chunk"]
                progress["chunk"] += 1
                s, ready, _ = where[chunks[c][0]]
                act.wait_ge(w_ready[s], ready)
                if c >= HIGHS:
                    act.wait_ge(*chunk_use[c - HIGHS])
                w_, high = chunk_views(c)
                st.done(A(rounded(high), w_, ACT.Copy), wh_ready)

            def square(k, first=False):
                if not first:
                    st.need(h_tile)
                st.done(A(SQ[:, k, :], H[:, k, :], ACT.Square), sq_ready)

            def split_input(x, n=T):
                for k in range(KD):
                    st.need(x_made)
                    st.done(A(rounded(SQ[:, k, 0:n]), x[:, k, 0:n], ACT.Copy), xh_ready)

            def deviation(out, b, eps, n, s):
                st.need(bank_full["act"][b])
                st.done(A(out, bank[b][:, 0:n], ACT.Sqrt, bias=const(eps)), s)

            def rms_norm(first=False):
                if first:
                    for k in range(KD):
                        square(k, True)
                deviation(RS[:, :], 7, "eps_rms", T, std_ready)

            def layer_norm(b):
                st.need(d2a)
                for k in range(KD):
                    st.done(A(SQ[:, k, 0:SEQ], R2[:, k, :], ACT.Square), sq_ready)
                deviation(RS[:, 0:SEQ], b + 1, "eps_ln", SEQ, std_ready)

            def ffn(first=False, dense_next=False):
                rms_norm(first)
                split_input(XN)
                if first:
                    for _ in range(HIGHS):
                        high_part()
                for f in range(NF):
                    pair = 2 * (f % 2)
                    if f >= 2:
                        st.need(hid_ready)
                    st.need(bank_full["act"][pair])
                    st.done(A(SG[:, f % 2, :], bank[pair][:, 0:T], ACT.Silu), silu_ready)
                    high_part()
                    high_part()
                st.need(hid_ready, 2)
                for j in range(16):
                    if j < 13 or dense_next:
                        high_part()
                    if j >= 3 and (j - 1) % 4 >= 2:
                        square((j - 1) // 4 * 2 + (j - 1) % 4 - 2)
                square(KD - 1)

            def gate_tile(l, g):
                b, at = 6 + g % 2, l * 16 + g
                st.need(bank_full["act"][b])
                st.done(A((GA, GB)[g // 8][:, g % 8, :], bank[b][:, 0:T], ACT.Sigmoid,
                          bias=small("bmerge")[:, at:at + 1]), bank_free["act"][b])

            def mixer(l):
                rms_norm()
                if l == 0:
                    act.wait_ge(tbl_w, 16)
                for i, b in ((4, 1), (5, 2)):
                    st.need(bank_full["act"][b])
                    st.done(A(S2[:, i, :], bank[b][:, 0:T], ACT.Square), a2d)
                st.need(bank_full["act"][3])
                st.done(A(VB[:, 0:2, :], bank[3][:, 0:256].rearrange("p (a b) -> p a b", a=2), ACT.Copy))
                st.done(A(VB[0:META, 2, :], bank[3][0:META, 256:384], ACT.Copy), bank_free["act"][3])
                for i in range(4):
                    st.need(bank_full["act"][4 + i])
                    st.done(A(S2[:, i, :], bank[4 + i][:, 0:T], ACT.Square), a2d)
                for m in range(4):
                    copy(QK[:, m, :], m, bank[m][:, 0:T])
                for i in range(6):
                    deviation(S2[:, i, :], i, "eps_rms", T, a2d)
                for t, (a_, nt) in enumerate(TILES):
                    b = (6, 7, 6)[t]
                    copy(VA[0:nt, t, :], b, bank[b][0:nt, :])
                st.need(d2a)
                st.done(A(EL, GT, ACT.Abs))
                st.settle()
                st.done(A(EL, EL, ACT.Exp, scale=-1.0))
                st.settle()
                st.done(A(EL, EL, ACT.Ln, bias=const("one")[:, 0:1]), a2d)
                for m in range(4):
                    b = (6, 7)[m % 2]
                    st.need(bank_full["act"][b])
                    st.done(A(RA[:, m, :], bank[b][:, 0:T], ACT.Silu), bank_free["act"][b])
                st.need(d2a)
                A(QD[:, 0], BC[:, 0:2, :], ACT.Exp)
                A(KI[:, 0], BC[:, 0:2, :], ACT.Exp, scale=-1.0)
                A(QD[:, 1], GT[:, 2:4, :], ACT.Exp)
                A(KI[:, 1], GT[:, 2:4, :], ACT.Exp, scale=-1.0)
                A(KE[:, 0], EL[:, 0:2, :], ACT.Exp)
                A(KE[:, 1], KE[:, 1], ACT.Exp)
                st.done(A(DEC, BC[:, :, 63:256:64], ACT.Exp), a2d)
                units = [(h, t) for h in range(8) for t in range(3)]
                for n in range(len(units) + 2):
                    if n < len(units):
                        h, t = units[n]
                        nt = TILES[t][1]
                        st.need(d2a)
                        st.done(A(PR[0:nt, n % 3, :], bank[n % 2][0:nt, 0:T], ACT.Exp,
                                  bias=ST1[0:nt, n % 8, 0:1], accum_out=ST1[0:nt, n % 8, 1:2]), a2d)
                    if n >= 2 and units[n - 2][1] == 2 and units[n - 2][0] % 2 == 1:
                        hp = units[n - 2][0] // 2
                        b = 4 + hp % 2
                        st.need(bank_full["act"][b])
                        st.done(A(BT[:, hp, :], bank[b][:, 0:T], ACT.Copy))
                        st.done(A(rounded(BTH[:, hp, :]), bank[b][:, 0:T], ACT.Copy), bank_free["act"][b])
                        mark(o_made)
                    if n - 1 in GATE_STEPS:
                        gate_tile(l, GATE_STEPS.index(n - 1))
                for _ in range(HIGHS):
                    high_part()
                for h in range(4):
                    st.need(bank_full["act"][2 + h])
                    st.done(A(SQ[:, h, :], bank[2 + h][:, 0:T], ACT.Square), sq_ready)
                for h in range(4):
                    deviation(SQ[:, 4 + h, :], (0, 1, 6, 7)[h], "eps_rms", T, a2d)
                for i in range(16):
                    high_part()
                    if i > KD:
                        square(i - KD - 1)
                square(KD - 1)

            def bias_rows():
                for h in range(NH2):
                    copy(BBUF[:, h, :], h % 2, bank[h % 2][:, 0:384])
                mark(tbl_row)

            def convolution():
                split_input(H, SEQ)
                for k in range(KD):
                    b = 3 * (k % 2) + 1
                    st.need(bank_full["act"][b])
                    if k >= 2:
                        st.need(d2a)
                    st.done(A(CV_C[:, k % 2, :], bank[b][:, 0:SEQ], ACT.Copy), bank_free["act"][b])
                    mark(a2d)
                    for _ in range(3):
                        high_part()
                st.need(d2a, 2)
                for _ in range(5):
                    high_part()

            def attention():
                st.need(x_made)
                st.done(A(rounded(SQ[:, :, 0:SEQ]), X2, ACT.Copy), xa_ready)
                st.need(d2a)
                st.done(A(LG2[:, 0, :], CK, ACT.Square), a2p)
                for m in range(4):
                    copy(QI[:, m, :], 3 + m, bank[3 + m][:, 0:SEQ])
                st.need(d2a)
                st.done(A(LG2[:, 1, :], KX, ACT.Square), a2p)
                deviation(LG2[:, 0, :], 0, "eps_rms", SEQ, a2d)
                deviation(LG2[:, 1, :], 1, "eps_ln", SEQ, a2d)
                copy(CKT, 2, bank[2][:, 0:SEQ].rearrange("p (a b) -> p a b", a=2))
                for _ in range(HIGHS):
                    high_part()
                for m in range(8):
                    copy(Q2[:, m, :], 3 + m % 4, bank[3 + m % 4][:, 0:SEQ])
                    high_part()
                for n in range(16):
                    ns = P * (n // 8 + 1)
                    st.need(bank_full["act"][n % 2])
                    st.done(A(RL[:, n % 2, 0:ns], bank[n % 2][:, 0:ns], ACT.Relu, scale=0.125), a2d)
                for m in range(8, 16):
                    copy(Q2[:, m, :], 3 + m % 4, bank[3 + m % 4][:, 0:SEQ])
                    high_part()
                units = [(h, t) for h in range(NH2) for t in range(2)]
                for n in range(len(units) + 3):
                    if n < len(units):
                        h, t = units[n]
                        ns = P * (t + 1)
                        st.need(d2a)
                        st.done(A(PR2[:, n % 3, 0:ns], LG2[:, n % 2, 0:ns], ACT.Exp,
                                  scale=-1.0, bias=ST2[:, n % 8, 1:2], accum_out=ST2[:, n % 8, 2:3]), a2d)
                    if 2 <= n < len(units) + 2:
                        m, t = n - 2, units[n - 2][1]
                        copy(PT2[:, m % 2, 0:t + 1, :], 2 + m % 2,
                             bank[2 + m % 2][:, 0:P * (t + 1)].rearrange("p (a b) -> p a b", b=P), a2p)
                    if n >= 3 and units[n - 3][1] == 1:
                        h = units[n - 3][0]
                        st.need(bank_full["act"][4 + h % 2])
                        st.done(A(O2[:, h, :], bank[4 + h % 2][:, 0:SEQ], ACT.Copy))
                        st.done(A(rounded(O2H[:, h, :]), bank[4 + h % 2][:, 0:SEQ], ACT.Copy),
                                bank_free["act"][4 + h % 2])
                        mark(o_made)
                for _ in range(13):
                    high_part()

            def experts(l):
                for q in range(4):
                    copy(XTOK[:, q // 2, (q % 2) * 512:(q % 2) * 512 + 512], 4 + q, bank[4 + q][:, :])
                for x in (E8, G8[:, 0:2, 0:1]):
                    st.need(d2a)
                    st.done(A(x, x, ACT.Exp), a2d)
                for q, b in ((0, 3), (1, 0)):
                    copy(ROWS[:, 2 * q:2 * q + 2, :], b, bank[b][:, :].rearrange("p (a b) -> p a b", a=2))
                mark(a2d)
                UP, TURN, DOWN = bank[4], bank[5], bank[6]
                m = M[l]

                def rows_out(b):
                    act.wait_ge(m.y, b + 1)
                    atleast(act, m.added, b)
                    A(YS[:, :], DOWN[:, :], ACT.Copy).then_inc(m.ys, 1)

                def group(i):
                    peeled = isinstance(i, int)
                    for u in range(GROUP):
                        b = GROUP * i + u
                        act.wait_ge(m.up, b + 1)
                        atleast(act, m.t, b)
                        A(HS[:, :], UP[:, :], ACT.Copy).then_inc(m.hs, 1)
                        if not (peeled and u == 0):
                            rows_out(b - 1)
                        act.wait_ge(m.t, b + 1)
                        atleast(act, m.ht, b)
                        A(SGM[:, :], TURN[:, 0:64], ACT.Silu).then_inc(m.sg, 1)

                group(0)
                rows_out(GROUP * own_and_more(act, l, group) - 1)
                for b in range(4):
                    copy(YT[:, b // 2, b % 2 * 512:b % 2 * 512 + 512], b, bank[b][:, :])

            act.wait_ge(loaded, 48)
            bias_rows()
            for l in range(2):
                ffn(first=(l == 0))
                mixer(l)
                ffn(dense_next=True)
            rms_norm()
            convolution()
            layer_norm(0)
            experts(0)
            layer_norm(0)
            attention()
            layer_norm(4)
            experts(1)
            layer_norm(0)

        @block.vector
        def _(dve):
            st = Steps(dve, dve_step)
            v = nc.vector
            TT, TS, STT = v.tensor_tensor, v.tensor_scalar, v.scalar_tensor_tensor

            def mark(s):
                st.settle()
                st.done(dve.nop(), s)

            def then(ins, s=None):
                st.done(ins, s)
                st.settle()

            def bcast(x, n):
                return x.unsqueeze(1).to_broadcast([x.shape[0], n, x.shape[1]])

            def inner(x, n):
                return x.unsqueeze(2).to_broadcast([x.shape[0], x.shape[1], n])

            def normed_and_split(gain, at, out, s, n=T):
                st.need(std_ready)
                then(v.reciprocal(RS[:, 0:n], RS[:, 0:n]))
                for k in range(KD + 1):
                    if k < KD:
                        st.done(STT(out[:, k, 0:n], H[:, k, 0:n], small(gain)[:, at + k:at + k + 1], RS[:, 0:n],
                                    ALU.mult, ALU.mult), x_made)
                    if k > 0:
                        st.need(xh_ready)
                        st.done(TT(rounded(XN[:, k - 1, 0:n]), out[:, k - 1, 0:n], part(SQ[:, k - 1, 0:n]),
                                   ALU.subtract), s)

            def normed(gain, at, out, s, n=T):
                st.need(std_ready)
                then(v.reciprocal(RS[:, 0:n], RS[:, 0:n]))
                for k in range(KD):
                    st.done(STT(out[:, k, 0:n], H[:, k, 0:n], small(gain)[:, at + k:at + k + 1], RS[:, 0:n],
                                ALU.mult, ALU.mult), s)

            def layer_norm(b, gain, bias, i):
                st.need(bank_full["dve"][b])
                st.done(TT(R2, R2, bcast(bank[b][:, 0:SEQ], KD), ALU.subtract), d2a)
                mark(bank_free["dve"][b])
                st.need(std_ready)
                then(v.reciprocal(RS[:, 0:SEQ], RS[:, 0:SEQ]))
                then(TT(R2, R2, bcast(RS[:, 0:SEQ], KD), ALU.mult))
                for k in range(KD):
                    at = i * KD + k
                    st.done(TS(X2[:, k, :], R2[:, k, :], small(gain)[:, at:at + 1], small(bias)[:, at:at + 1],
                               ALU.mult, ALU.add), x_tile)

            def sum_from(b, k):
                st.need(bank_full["dve"][b])
                st.done(STT(R2[:, k, :], X2[:, k, :], ALPHA, bank[b][:, 0:SEQ], ALU.mult, ALU.add), sum_tile)
                mark(bank_free["dve"][b])

            def ffn(l, j):
                normed_and_split("gains", (l * 3 + 2 * j) * KD, XN, xn_ready)
                for f in range(NF):
                    b = 2 * (f % 2) + 1
                    st.need(silu_ready)
                    st.need(bank_full["dve"][b])
                    st.done(TT(HID[:, f, :], SG[:, f % 2, :], bank[b][:, 0:T], ALU.mult))
                    then(TT(rounded(HIDH[:, f, :]), SG[:, f % 2, :], bank[b][:, 0:T], ALU.mult))
                    st.done(TT(rounded(HID[:, f, :]), HID[:, f, :], part(HIDH[:, f, :]), ALU.subtract), hid_ready)
                for c in range(4):
                    for dt in range(2):
                        b, k = (4 if c % 2 == 0 else 0) + dt, 2 * c + dt
                        st.need(bank_full["dve"][b])
                        st.done(STT(H[:, k, :], bank[b][:, 0:T], 0.5, H[:, k, :], ALU.mult, ALU.add), h_tile)
                        mark(bank_free["dve"][b])

            def mixer(l):
                normed("gains", (l * 3 + 1) * KD, XN, xn_ready)
                if l == 0:
                    dve.wait_ge(tbl_w, 16)
                st.need(bank_full["dve"][0])
                st.done(v.tensor_copy(LR[0:16, :], bank[0][0:16, 0:T]))
                st.done(v.tensor_copy(LR[32:48, :], bank[0][32:48, 0:T]), bank_free["dve"][0])
                for i, b in ((4, 1), (5, 2), (0, 4), (1, 5), (2, 6), (3, 7)):
                    st.need(a2d)
                    st.done(v.tensor_copy(QB[:, i, :], bank[b][:, 0:T]), bank_free["dve"][b])
                for i in range(4):
                    st.need(bank_full["dve"][4 + i])
                    st.done(TS(GT[:, i, :], bank[4 + i][:, 0:T], small("gla_b")[:, l * 4 + i:l * 4 + i + 1], None,
                               ALU.add), bank_free["dve"][4 + i])
                st.settle()
                st.done(TS(BC, GT, 0.0, None, ALU.min), d2a)
                for i in range(6):
                    st.need(a2d)
                    then(v.reciprocal(S2[:, i, :], S2[:, i, :]))
                    g = small("qn" if i < 4 else "kn")[:, l:l + 1]
                    st.done(STT(XR[:, i, :], QB[:, i, :], g, S2[:, i, :], ALU.mult, ALU.mult), d2p)
                st.settle()
                for i in range(6):
                    cos, sin = (const("cosq"), const("sinq")) if i < 4 else (const("cos"), const("sin"))
                    st.done(TT(QR[:, i, :], XR[:, i, :], cos, ALU.mult))
                    st.need(bank_full["dve"][i])
                    then(TT(QB[:, i, :], bank[i][:, 0:T], sin, ALU.mult), bank_free["dve"][i])
                    st.done(TT(QR[:, i, :], QR[:, i, :], QB[:, i, :], ALU.add), None if i < 5 else d2p)
                st.need(a2d)
                then(TT(GT, BC, EL, ALU.subtract))
                then(TS(GT, GT, 1.0 / 16.0, None, ALU.mult))
                for i in range(4):
                    st.done(v.tensor_tensor_scan(BC[:, i, :], const("restart"), GT[:, i, :], 0.0, ALU.mult, ALU.add))
                st.settle()

                def chunks(x):
                    return x[:, 0:SEQ].rearrange("p (c n) -> p c n", c=4)

                for i in range(4):
                    total = BC[:, i, 63:256:64].unsqueeze(2).to_broadcast([P, 4, 64])
                    st.done(TT(chunks(EL[:, i, :]), total, chunks(BC[:, i, :]), ALU.subtract))
                    st.done(TT(EL[:, i, SEQ:T], BC[:, i, T - 1:T].to_broadcast([P, META]), BC[:, i, SEQ:T],
                               ALU.subtract))
                then(TT(KE[:, 1], BC[:, 2:4, :], GT[:, 2:4, :], ALU.subtract))
                st.done(TT(GT[:, 2:4, :], EL[:, 2:4, :], GT[:, 2:4, :], ALU.add), d2a)
                st.need(a2d)
                for d in range(2):
                    st.done(STT(QD[:, d], QD[:, d], 0.125, QK[:, 0:2, :], ALU.mult, ALU.mult))
                    st.done(TT(KI[:, d], KI[:, d], QK[:, 2:4, :], ALU.mult))
                    st.done(TT(KE[:, d], KE[:, d], QK[:, 2:4, :], ALU.mult), gla_ready if d else None)
                units = [(h, t) for h in range(8) for t in range(3)]
                for n in range(len(units) + 2):
                    if n < len(units):
                        nt, s = TILES[units[n][1]][1], n % 8
                        st.need(bank_full["dve"][n % 2])
                        st.done(v.tensor_reduce(ST1[0:nt, s, 0:1], bank[n % 2][0:nt, 0:T], AX.X, ALU.max,
                                                negate=True), d2a)
                    if 1 <= n <= len(units):
                        m = n - 1
                        nt, s = TILES[units[m][1]][1], m % 8
                        st.need(a2d)
                        then(v.reciprocal(ST1[0:nt, s, 2:3], ST1[0:nt, s, 1:2]), bank_free["dve"][m % 2])
                        st.done(TS(PR[0:nt, m % 3, :], PR[0:nt, m % 3, :], ST1[0:nt, s, 2:3], None, ALU.mult), d2p)
                    if n >= 2:
                        m = n - 2
                        nt, b = TILES[units[m][1]][1], 2 + m % 2
                        st.need(bank_full["dve"][b])
                        src = bank[b][:, 0:256].rearrange("p (a b) -> p a b", a=2)
                        st.done(v.tensor_copy(PT[:, m % 2, 0:2, 0:nt], src[:, :, 0:nt]))
                        st.done(v.tensor_copy(PT[0:META, m % 2, 2, 0:nt], bank[b][0:META, 256:256 + nt]), d2p)
                for t, (c, nt) in enumerate(TILES):
                    st.need(bank_full["dve"][t])
                    st.done(v.tensor_copy(KET[0:nt, t], bank[t][0:nt, :].rearrange("p (a b) -> p a b", a=2)),
                            bank_free["dve"][t])
                for d, m in enumerate(("low", "high")):
                    st.need(bank_full["dve"][3 + d])
                    st.done(TT(ATT[:, d], bank[3 + d][:, :].rearrange("p (a b) -> p a b", a=8), bcast(const(m), 8),
                               ALU.mult), bank_free["dve"][3 + d])
                st.need(bank_full["dve"][5])
                for d, m in enumerate(("low", "high")):
                    st.done(TT(ATM[0:META, d].rearrange("p (a b) -> p a b", a=4),
                               bank[5][0:META, d * 64:d * 64 + 64].rearrange("p (a b) -> p a b", a=4),
                               bcast(const(m, META)[:, 0:META], 4), ALU.mult), bank_free["dve"][5] if d else None)
                for s in range(4):
                    for d in range(2):
                        b, q = (6 + s // 2, s % 2) if d == 0 else (s // 2, s % 2)
                        if q == 0:
                            st.need(bank_full["dve"][b])
                        src = bank[b][:, q * 256:q * 256 + 256]
                        free = bank_free["dve"][b] if q == 1 else None
                        if s == 0:
                            st.done(v.tensor_copy(ST[:, d, 0, :], src))
                        else:
                            c = s - 1 if d == 0 else 3 - s
                            for tile in range(2):
                                cs = slice(tile * P, tile * P + P)
                                st.done(STT(ST[:, d, s, cs], ST[:, d, s - 1, cs], DEC[:, 2 * d + tile, c:c + 1],
                                            src[:, cs], ALU.mult, ALU.add), free if tile else None)
                    st.settle()
                for h in range(4):
                    st.need(a2d)
                    then(v.reciprocal(SQ[:, 4 + h, :], SQ[:, 4 + h, :]))
                    g = small("gla_gn")[:, l * 4 + h:l * 4 + h + 1]
                    then(STT(AT[:, h, :], bank[2 + h][:, 0:T], g, SQ[:, 4 + h, :], ALU.mult, ALU.mult),
                         bank_free["dve"][2 + h])
                    then(TT(rounded(ATH[:, h, :]), AT[:, h, :], RA[:, h, :], ALU.mult))
                    then(TT(AT[:, h, :], AT[:, h, :], RA[:, h, :], ALU.mult))
                    st.done(TT(rounded(AT[:, h, :]), AT[:, h, :], part(ATH[:, h, :]), ALU.subtract),
                            None if h < 3 else d2p)
                for k in range(KD):
                    b = 2 * (k % 2)
                    st.need(bank_full["dve"][b])
                    st.done(TT(GA[:, k, :], GA[:, k, :], bank[b][:, 0:T], ALU.mult), bank_free["dve"][b])
                    st.need(bank_full["dve"][b + 1])
                    then(TT(GB[:, k, :], GB[:, k, :], bank[b + 1][:, 0:T], ALU.mult), bank_free["dve"][b + 1])
                    then(TT(GA[:, k, :], GA[:, k, :], GB[:, k, :], ALU.add))
                    then(v.tensor_copy(rounded(GAH[:, k, :]), GA[:, k, :]))
                    st.done(TT(rounded(GA[:, k, :]), GA[:, k, :], part(GAH[:, k, :]), ALU.subtract),
                            None if k < KD - 1 else d2p)
                for k in range(KD):
                    b = 4 + k % 4
                    st.need(bank_full["dve"][b])
                    st.done(TT(H[:, k, :], bank[b][:, 0:T], H[:, k, :], ALU.add), h_tile)
                    mark(bank_free["dve"][b])

            def bias_rows():
                for h in range(NH2):
                    st.done(TS(BROW[0:32, h, :], const("onehot", 32), small("rel", 32)[:, h:h + 1], None, ALU.mult),
                            d2p)

            def convolution():
                st.done(v.memset(CV_U[:, :, 0:2], 0.0))
                for k in range(KD):
                    u, o, t0 = CV_U[:, k % 2, :], CV_V[:, k, :], CV_T[:, k % 2, :]
                    b = 3 * (k % 2)
                    w_ = [small("convk")[:, j * KD + k:j * KD + k + 1] for j in range(3)]
                    st.need(a2d)
                    st.need(bank_full["dve"][b + 2])
                    then(TT(u[:, 2:SEQ + 2], CV_C[:, k % 2, :], bank[b + 2][:, 0:SEQ], ALU.mult),
                         bank_free["dve"][b + 2])
                    mark(d2a)
                    then(TS(t0, u[:, 0:SEQ], w_[0], None, ALU.mult))
                    then(STT(t0, u[:, 1:SEQ + 1], w_[1], t0, ALU.mult, ALU.add))
                    then(STT(t0, u[:, 2:SEQ + 2], w_[2], t0, ALU.mult, ALU.add))
                    st.need(bank_full["dve"][b])
                    st.done(TT(o, t0, bank[b][:, 0:SEQ], ALU.mult))
                    then(TT(rounded(CV_H[:, k, :]), t0, bank[b][:, 0:SEQ], ALU.mult), bank_free["dve"][b])
                    st.done(TT(rounded(o), o, part(CV_H[:, k, :]), ALU.subtract), d2p)
                for k in range(KD):
                    sum_from(6 + k % 2, k)

            def attention():
                mark(x_made)
                st.need(bank_full["dve"][0])
                st.done(v.tensor_copy(CK, bank[0][:, 0:SEQ]), d2a)
                mark(bank_free["dve"][0])
                st.need(bank_full["dve"][1])
                st.done(v.tensor_copy(KX, bank[1][:, 0:SEQ]), d2p)
                mark(bank_free["dve"][1])
                st.need(bank_full["dve"][2])
                st.done(TS(WI, bank[2][:, 0:16].rearrange("p (a b) -> p a b", a=2), 8.0 ** -0.5, None, ALU.mult),
                        bank_free["dve"][2])
                st.need(bank_full["dve"][7])
                st.done(TT(KX, KX, bank[7][:, 0:SEQ], ALU.subtract), d2a)
                mark(bank_free["dve"][7])
                st.need(a2d)
                then(v.reciprocal(LG2[:, 0, :], LG2[:, 0, :]))
                st.done(STT(CKN, CK, small("kvg"), LG2[:, 0, :], ALU.mult, ALU.mult), d2p)
                st.need(a2d)
                then(v.reciprocal(LG2[:, 1, :], LG2[:, 1, :]))
                then(TT(KN2, KX, LG2[:, 1, :], ALU.mult))
                st.done(TS(KN2, KN2, small("kig"), small("kib"), ALU.mult, ALU.add), d2p)
                for n in range(16):
                    t, h = n // 8, n % 8
                    ns = P * (t + 1)
                    sc = SC[:, t, 0:ns]
                    acc = const("future").rearrange("p (a b) -> p a b", a=2)[:, t, 0:ns] if h == 0 else sc
                    st.need(a2d)
                    then(STT(sc, RL[:, n % 2, 0:ns], WI[:, t, h:h + 1], acc, ALU.mult, ALU.add),
                         bank_free["dve"][n % 2])
                for t in range(2):
                    ns = P * (t + 1)
                    sc, wk = SC[:, t, 0:ns], WK[:, t, 0:ns]
                    for r in range(TOPK // 8):
                        src = sc if r == 0 else wk
                        then(v.max(M8, src))
                        then(v.match_replace(wk, M8, src, LOWEST))
                    m = MSK[:, t, 0:ns]
                    then(TT(m, wk, sc, ALU.not_equal))
                    then(TT(m, m, const("causal").rearrange("p (a b) -> p a b", a=2)[:, t, 0:ns], ALU.mult))
                    then(TS(m, m, -BIG, BIG, ALU.mult, ALU.add))
                dve.wait_ge(tbl_r, 16 * 8)
                units = [(h, t) for h in range(NH2) for t in range(2)]
                for n in range(len(units) + 1):
                    if n < len(units):
                        h, t = units[n]
                        ns, s = P * (t + 1), n % 8
                        lg = LG2[:, n % 2, 0:ns]
                        st.need(bank_full["dve"][n % 2])
                        st.done(STT(lg, bank[n % 2][:, 0:ns], -P ** -0.5, (BIAS0, BIAS1)[t][:, h, :],
                                    ALU.mult, ALU.subtract), bank_free["dve"][n % 2])
                        biased = st.last
                    if n >= 1:
                        m = n - 1
                        ms, r = P * (units[m][1] + 1), m % 8
                        st.need(a2d)
                        st.done(v.reciprocal(ST2[:, r, 3:4], ST2[:, r, 2:3]))
                        inverse = st.last
                    if n < len(units):
                        dve.wait_ge(*biased)
                        st.done(v.tensor_tensor_reduce(out=lg, in0=lg, in1=MSK[:, t, 0:ns], scale=1.0,
                                                       scalar=-LOWEST, op0=ALU.add, op1=ALU.min,
                                                       accum_out=ST2[:, s, 1:2]), d2a)
                    if n >= 1:
                        dve.wait_ge(*inverse)
                        st.done(TS(PR2[:, m % 3, 0:ms], PR2[:, m % 3, 0:ms], ST2[:, r, 3:4], None, ALU.mult), d2p)
                for k in range(KD):
                    sum_from(6 + k % 2, k)

            def first_best(x, best, out, scr):
                then(v.tensor_reduce(best, x, AX.X, ALU.max))
                then(TT(scr, x, best.to_broadcast([P, 2, 8]), ALU.is_ge))
                then(TT(scr, scr, bcast(const("rev8"), 2), ALU.mult))
                then(v.tensor_reduce(G8[:, 0:2, 1:2], scr, AX.X, ALU.max))
                then(TT(out, scr, G8[:, 0:2, 1:2].to_broadcast([P, 2, 8]), ALU.is_equal))

            def experts(l):
                rb = small("rb")[:, l * 72:l * 72 + 72]
                gmax, v1, v2 = SLT[:, 0:2, 0:1], SLT[:, 2:4, 0:1], SLT[:, 4:6, 0:1]
                gsum = SLT[:, 6:8, 0:1]
                pay1, pay2 = SLT[:, 0:2, 1:2], SLT[:, 2:4, 1:2]
                slots = SLT[:, 4:8, 1:2]
                exv = G8[:, 0:2, 0:1]
                scr = G8[:, 2:4, :]
                st.need(bank_full["dve"][0])
                then(TT(LG, bank[0][:, 0:144].rearrange("p (a b) -> p a b", a=2), bcast(rb, 2), ALU.add),
                     bank_free["dve"][0])
                first_best(LG[:, :, 0:8], gmax, OHG, SCR8)
                st.done(TT(E8, LG[:, :, 0:8], gmax.to_broadcast([P, 2, 8]), ALU.subtract), d2a)
                for t in range(2):
                    e = LG[:, t, 8:72].rearrange("p (g e) -> p g e", g=8)
                    tm = TMP[:, t, :].rearrange("p (g e) -> p g e", g=8)
                    then(TT(tm, e, inner(OHG[:, t, :], 8), ALU.mult))
                    then(v.tensor_reduce(ES[:, t, :].unsqueeze(2), TMP[:, t, :].rearrange("p (g e) -> p e g", g=8),
                                         AX.X, ALU.add))
                first_best(ES, v1, OH[:, 0], SCR8)
                then(STT(ES, OH[:, 0], -BIG, ES, ALU.mult, ALU.add))
                first_best(ES, v2, OH[:, 1], SCR8)
                st.need(a2d)
                then(v.tensor_reduce(gsum, E8, AX.X, ALU.add))
                then(v.reciprocal(gsum, gsum))
                st.done(TT(exv, v2, v1, ALU.subtract), d2a)
                st.need(a2d)
                then(TS(pay1, exv, 1.0, None, ALU.add))
                then(v.reciprocal(pay1, pay1))
                then(TT(pay1, pay1, gsum, ALU.mult))
                then(TT(pay2, exv, pay1, ALU.mult))
                for a_ in range(2):
                    for t in range(2):
                        then(TT(MA[:, a_, t, :].rearrange("p (g e) -> p g e", g=8), inner(OHG[:, t, :], 8),
                                bcast(OH[:, a_, t, :], 8), ALU.mult))
                st.done(TT(MA[:, 2], MA[:, 0], MA[:, 1], ALU.add), d2p)
                st.need(bank_full["dve"][1])
                then(TT(CMP, inner(bank[1][:, 128:192], 8), bcast(const("steps8"), 64), ALU.is_gt))
                then(v.tensor_reduce(CNT[:, 0, :].unsqueeze(2), CMP, AX.X, ALU.add))
                then(v.tensor_tensor_scan(CNT[:, 1, :], const("one"), CNT[:, 0, :], 0.0, ALU.mult, ALU.add))
                then(TT(CNT[:, 3, :], CNT[:, 1, :], const("ident")[:, 0:64], ALU.mult))
                then(v.tensor_reduce(CNT[:, 4, 0:1], CNT[:, 3, :], AX.X, ALU.add))
                st.done(TS(CMB[0:64, :], const("blocks", 64), CNT[0:64, 4, 0:1], None, ALU.is_ge), d2p)
                then(TT(CNT[:, 2, :], CNT[:, 1, :], CNT[:, 0, :], ALU.subtract))
                then(STT(CNT[:, 2, :], CNT[:, 2, :], float(SLOTS), const("late"), ALU.mult, ALU.add))
                for t in range(2):
                    rank = bank[1][:, t * 64:t * 64 + 64]
                    then(STT(RK[:, t, :], rank, float(SLOTS), CNT[:, 2, :], ALU.is_ge, ALU.mult))
                    then(TT(RK[:, t, :], RK[:, t, :], rank, ALU.add))
                    then(TT(RK[:, t, :], RK[:, t, :], const("first"), ALU.add))
                then(TS(CNT[:, 4, 4:8], const("groups"), CNT[:, 1, NE - 1:NE], None, ALU.is_lt))
                then(v.tensor_reduce(CNT[:, 4, 8:9], CNT[:, 4, 4:8], AX.X, ALU.add))
                mark(bank_free["dve"][1])
                for a_ in range(2):
                    then(TT(TMP, MA[:, a_], RK, ALU.mult))
                    then(v.tensor_reduce(slots[:, 2 * a_:2 * a_ + 2], TMP, AX.X, ALU.add))
                for i in range(8):
                    x = (slots[:, 0:2], slots[:, 2:4], pay1, pay2)[i // 2][:, i % 2, :]
                    st.done(TS(DG[:, i, :], const("ident"), x, None, ALU.mult), d2p if i == 7 else None)
                st.need(bank_full["dve"][2])
                st.done(TS(IDS[0:1, 0:MORE], bank[2][0:1, 0:MORE], float(NE - 1), None, ALU.min))
                st.done(v.tensor_copy(IDS[0:1, MORE:MORE + 1], CNT[0:1, 4, 8:9]), ids_ready)
                st.settle()
                mark(bank_free["dve"][2])
                then(v.tensor_copy(SLC.unsqueeze(2), slots))
                for u in range(GROUP):
                    then(TS(PC[:, u:u + 1], const("row32"), float(SLOTS * u), None, ALU.add))
                st.need(a2d)
                TURN, GATHER = bank[5], bank[7]
                m = M[l]

                def select(i, done_before):
                    atleast(dve, m.ss, done_before)
                    atleast(dve, m.g_full, 2 * i)
                    for t in range(2):
                        TS(GS[:, t, :], const("iota"), SLC[:, t:t + 1], None, ALU.is_equal).then_inc(m.ss, 1)
                    dve.wait_ge(m.ss, done_before + 2)
                    for t in range(2):
                        ins = STT(GS[:, t, :], const("iota"), SLC[:, 2 + t:3 + t], GS[:, t, :], ALU.is_equal, ALU.add)
                    ins.then_inc(m.sel, 1)
                    dve.wait_ge(m.sel, i + 1)
                    TS(SLC, SLC, float(-GROUP * SLOTS), None, ALU.add).then_inc(m.ss, 1)

                select(0, 0)

                def group(i):
                    for half in range(2):
                        dve.wait_ge(m.g_full, 2 * i + half + 1)
                        if half == 0:
                            atleast(dve, m.up, GROUP * i)
                        v.tensor_copy(XG[:, 4 * half:4 * half + 4, :],
                                      GATHER[:, :].rearrange("p (a b) -> p a b", a=4)).then_inc(m.xg, 1)
                    select(i + 1, 3 + 4 * i)
                    for u in range(GROUP):
                        b = GROUP * i + u
                        atleast(dve, m.added, b - 1)
                        o = PUT[:, u % 2, :]
                        STT(o, ROWS[:, 0, :], PC[:, u:u + 1], ROWS[:, 2, :], ALU.is_equal, ALU.mult).then_inc(m.ps, 1)
                        atleast(dve, m.put, b)
                        STT(PUT2, ROWS[:, 1, :], PC[:, u:u + 1], ROWS[:, 3, :], ALU.is_equal, ALU.mult).then_inc(m.ps, 1)
                        dve.wait_ge(m.ps, 2 * b + 2)
                        TT(o, o, PUT2, ALU.add).then_inc(m.put, 1)
                        dve.wait_ge(m.sg, b + 1)
                        atleast(dve, m.y, b)
                        TT(HT, SGM, TURN[:, 64:128], ALU.mult).then_inc(m.ht, 1)
                    dve.wait_ge(m.put, GROUP * i + GROUP)
                    TS(PC, PC, float(GROUP * SLOTS), None, ALU.add).then_inc(m.ss, 1)

                group(0)
                own_and_more(dve, l, group)
                for k in range(KD):
                    sum_from(4 + k % 4, k)

            dve.wait_ge(loaded, 48)
            bias_rows()
            for l in range(2):
                ffn(l, 0)
                mixer(l)
                ffn(l, 1)
            normed_and_split("final", 0, H, x_tile, SEQ)
            convolution()
            layer_norm(0, "ln1g", "ln1b", 0)
            experts(0)
            layer_norm(0, "ln2g", "ln2b", 0)
            x_at["attention"] = st.sent[x_tile]
            attention()
            layer_norm(4, "ln1g", "ln1b", 1)
            experts(1)
            layer_norm(0, "ln2g", "ln2b", 1)
            x_at["end"] = st.sent[x_tile]

        @block.gpsimd
        def _(pool):
            skew = P * 513
            pool.wait_ge(tbl_row, 1)
            pool.dma_start(table_dram[:, 0:skew].rearrange("h (p x) -> p h x", x=513)[:, :, 0:384], BBUF
                           ).then_inc(tbl_w, 16)
            pool.wait_ge(tbl_w, 16)
            st = Steps(pool, None)

            def low_parts(first, n):
                for c in range(first, first + n):
                    low, high = chunk_views(c)
                    pool.wait_ge(wh_ready, c + 1)
                    st.done(nc.gpsimd.tensor_tensor(rounded(low), low, part(high), ALU.subtract), wl_ready)

            n_q, n_out = (len([c for c in chunks if c[0][0] == kind]) for kind in ("d_q", "d_out"))
            at = len(chunks) - n_q - n_out

            def low_outputs(o, high, n):
                for h in range(n):
                    st.need(o_made)
                    st.done(nc.gpsimd.tensor_tensor(rounded(o[:, h, :]), o[:, h, :], part(high[:, h, :]),
                                                    ALU.subtract), xl_ready)

            done = 0
            for l in range(2):
                n_ffn = len([c for c in chunks if c[0][0] in ("up", "down") and c[0][1:3] == (l, 0)])
                low_parts(done, n_ffn)
                low_outputs(BT, BTH, 4)
                n_mixer = len([c for c in chunks if c[0][0] in ("pa", "pb", "out") and c[0][1] == l])
                low_parts(done + n_ffn, n_mixer + n_ffn)
                done += 2 * n_ffn + n_mixer
            low_parts(done, at - done)
            pool.wait_ge(x_tile, x_at["attention"])
            for h in range(0, NH2, 4):
                for t, dst in ((0, BIAS0), (1, BIAS1)):
                    n = P * (t + 1)
                    src = table_dram[h:h + 4, 0:P * 512].rearrange("h (p x) -> p h x", x=512)
                    pool.dma_start(dst[:, h:h + 4, :], src[:, :, 255 - P * t:255 - P * t + n]).then_inc(tbl_r, 16)
            st.need(xa_ready)
            st.done(nc.gpsimd.tensor_tensor(rounded(R2), X2, part(SQ[:, :, 0:SEQ]), ALU.subtract), xl_ready)
            low_parts(at, n_q + HIGHS)
            low_outputs(O2, O2H, NH2)
            low_parts(at + n_q + HIGHS, n_out - HIGHS)

        @block.sync
        def _(sp):
            sp.dma_start(CST[:, :], cst_dram).then_inc(loaded, 16)
            sp.dma_start(SM[:, :], small_dram).then_inc(loaded, 16)
            sp.dma_start(H[:, :, :], h0_dram).then_inc(loaded, 16)

            def load_w13(l, u, e):
                v = RING_B[u][:, 0:SLOT].rearrange("p (k m n) -> p k m n", k=KD, m=2)
                for j, name in enumerate(("exp_w1_2", "exp_w3_2")):
                    sp.dma_start(v[:, :, j, :], w[name][l][bass.ds(e, 1)].rearrange("o (k p) n -> p (o k) n", p=P)
                                 ).then_inc(M[l].w13[u], 16)

            def load_w2(l, u, e):
                sp.dma_start(W2B[:, u, :].rearrange("p (k n) -> p k n", k=2),
                             w["exp_w2_2"][l][bass.ds(e, 1)].rearrange("o (k p) n -> p (o k) n", p=P)
                             ).then_inc(M[l].w2[u], 16)

            def expert_weights(l, i, own):
                for u in range(GROUP):
                    b = GROUP * i + u
                    e = b if own else sp.value_load(IDS[0:1, bass.ds(b - NE, 1)], min_val=0, max_val=NE - 1)
                    sp.wait_ge(M[l].up, b - GROUP + 1)
                    load_w13(l, u, e)
                    sp.wait_ge(M[l].y, b - GROUP + 1)
                    load_w2(l, u, e)

            done_moe = 0
            for label, view in plan:
                s, _, before = where[label]
                if view is None:
                    l = label[1]
                    sp.dma_start(RW[:, :, 0:8], w["router_wg_2"][l].rearrange("(k p) n -> p k n", p=P)
                                 ).then_inc(rw_ready, 16)
                    sp.dma_start(RW[:, :, 8:72], w["router_we_2"][l].rearrange("(k p) n -> p k n", p=P)
                                 ).then_inc(rw_ready, 16)
                    first = before
                    for u in range(GROUP):
                        sp.wait_ge(*last_use[first[u]])
                        load_w13(l, u, u)
                    if l == 0:
                        sp.wait_ge(*last_use["down", 1, 1, 3, 1])
                    for u in range(GROUP):
                        load_w2(l, u, u)
                    with sp.Fori(1, NG0) as i:
                        expert_weights(l, i, own=True)
                    sp.wait_ge(ids_ready, l + 1)
                    n = NG0 + sp.value_load(IDS[0:1, MORE:MORE + 1], min_val=0, max_val=NG - NG0)
                    with sp.Fori(NG0, NG) as i:
                        with sp.If(i < n):
                            expert_weights(l, i, own=False)
                    sp.wait_ge(M[l].y, GROUP * n)
                    continue
                if before is not None:
                    sp.wait_ge(*last_use[before])
                for dst, src in view(RING_B[s]):
                    sp.dma_start(dst, src).then_inc(w_ready[s], 16)
            sp.wait_ge(x_tile, x_at["end"])
            sp.dma_start(out_dram, X2).then_inc(stored, 16)
            sp.wait_ge(stored, 16)


BIG_INPUTS = ["ffn_w_gate", "ffn_w_up", "ffn_w_down", "w_in", "w_pa", "w_pb", "w_out", "conv_w_in_2", "conv_w_out_2",
              "attn_w_in_2", "attn_w_out_2", "router_wg_2", "router_we_2", "exp_w1_2", "exp_w3_2", "exp_w2_2"]


def pack_smalls(x):
    s = small_layout()
    out = np.zeros((P, s.n), np.float32)

    def put(name, v):
        a, n = s.at[name]
        out[:v.shape[0], a:a + n] = v

    def tiles(v):
        return np.asarray(v).reshape(-1, P).T

    def twice(v):
        return np.concatenate([v, v], axis=-1).T

    put("gains", tiles(x["norm_gains"]))
    put("final", tiles(x["final_norm"]))
    put("gla_b", tiles(x["gla_b2"]))
    put("gla_gn", tiles(x["gla_gn"]))
    put("qn", twice(x["q_norm"]))
    put("kn", twice(x["k_norm"]))
    put("bmerge", tiles(x["b_merge"]))
    put("convk", tiles(x["conv_k_2"]))
    put("kvg", tiles(x["kv_norm_g_2"]))
    put("kig", twice(x["kidx_ln_g_2"]))
    put("kib", twice(x["kidx_ln_b_2"]))
    rb = np.concatenate([x["router_bg_2"], x["router_be_2"]], axis=1).reshape(1, 144)
    put("rb", np.broadcast_to(rb, (P, 144)))
    for name in ("ln1g", "ln1b", "ln2g", "ln2b"):
        put(name, tiles(x[f"{name[:3]}_{name[3]}_2"]))
    put("rel", x["rel_bias_2"])
    a, _ = s.at["gla_w"]
    for l in range(2):
        for d in range(2):
            out[32 * d:32 * d + 16, a + l * 256:a + l * 256 + 256] = x["gla_w2"][l, d]
    return out


def kernel(**inputs):
    import concourse.bacc as bacc
    from concourse.bass_utils import run_bass_kernel_spmd

    x = {k: np.asarray(v) for k, v in inputs.items()}
    nc = bacc.Bacc("TRN2", target_bir_lowering=False, num_devices=1)
    h0 = np.concatenate([x["x"][0], x["meta_tokens"]], axis=0).T.reshape(KD, P, T).transpose(1, 0, 2)
    arrays = {"cst": constants(), "smalls": pack_smalls(x), "h0": np.ascontiguousarray(h0)}
    arrays.update({f"in_{n}": np.ascontiguousarray(x[n]) for n in BIG_INPUTS})
    drams = {n: nc.dram_tensor(n, a.shape, F32, kind="ExternalInput").ap() for n, a in arrays.items()}
    w = {n: drams[f"in_{n}"] for n in BIG_INPUTS}
    table = nc.dram_tensor("bias_table", (NH2, P * 513), F32, kind="Internal").ap()
    out = nc.dram_tensor("out", (P, KD, SEQ), F32, kind="ExternalOutput").ap()
    build_model(nc, w, drams["cst"], drams["smalls"], drams["h0"], table, out)
    r = run_bass_kernel_spmd(nc, [arrays], core_ids=[0])
    got = np.asarray(r.results[0]["out"])
    return np.ascontiguousarray(got.transpose(2, 1, 0).reshape(1, SEQ, D))
```
